# Optimizing a Trainium2 kernel written in Bass

```python
import jax, jax.numpy as jnp
from jax import lax
import numpy as np

D_MODEL = 1024
BATCH = 1
SEQ = 2048
DEPTH = 1

GRID_W = 64
Q_BLOCK = 128
ROPE_THETA = 10000.0
EPS = 1e-6
D_MIX = D_MODEL
A_HEAD_DIM = 64
A_WIDTH = D_MIX // 2
A_HEADS = A_WIDTH // A_HEAD_DIM
A_KV_HEADS = 2
B_WIDTH = D_MIX - A_WIDTH
B_V_HEAD_DIM = 128
B_HEADS = B_WIDTH // B_V_HEAD_DIM
B_NOPE_DIM = 64
B_ROPE_DIM = 32
B_QK_DIM = B_NOPE_DIM + B_ROPE_DIM
B_Q_RANK = 384
B_KV_RANK = 256

_SIZES = (
    A_WIDTH,
    A_KV_HEADS * A_HEAD_DIM,
    A_KV_HEADS * A_HEAD_DIM,
    A_WIDTH,
    B_Q_RANK,
    B_KV_RANK,
    B_ROPE_DIM,
    B_WIDTH,
)
N_IN = int(sum(_SIZES))
_SPLITS = tuple(int(v) for v in np.cumsum(_SIZES)[:-1])

kernel_name = "hybrid_gqa_mla_parallel_groups"

def rms_norm(x, g):
    xf = x.astype(jnp.float32)
    y = xf * lax.rsqrt(jnp.mean(xf * xf, axis=-1, keepdims=True) + EPS)
    return (y * g.astype(jnp.float32)).astype(x.dtype)

def axial_rope_tables(seq_len, dim):
    rows = seq_len // GRID_W
    row = jnp.repeat(jnp.arange(rows, dtype=jnp.float32), GRID_W)
    col = jnp.tile(jnp.arange(GRID_W, dtype=jnp.float32), rows)
    half = dim // 2
    inv = 1.0 / (ROPE_THETA ** (jnp.arange(0, half, 2, dtype=jnp.float32) / half))
    ang_r = row[:, None] * inv[None, :]
    ang_c = col[:, None] * inv[None, :]
    return jnp.cos(ang_r), jnp.sin(ang_r), jnp.cos(ang_c), jnp.sin(ang_c)

def _rotate(xh, cos, sin):
    x1, x2 = jnp.split(xh, 2, axis=-1)
    return jnp.concatenate([x1 * cos - x2 * sin, x1 * sin + x2 * cos], axis=-1)

def apply_axial_rope(x, tables):
    cr, sr, cc, sc = tables
    xf = x.astype(jnp.float32)
    xr, xc = jnp.split(xf, 2, axis=-1)
    out = jnp.concatenate([_rotate(xr, cr, sr), _rotate(xc, cc, sc)], axis=-1)
    return out.astype(x.dtype)

def blocked_attention(q, k, v):
    bsz, n_heads, s_len, dk = q.shape
    n_kv = k.shape[1]
    grp = n_heads // n_kv
    dv = v.shape[-1]
    nb = s_len // Q_BLOCK
    scale = 1.0 / float(np.sqrt(dk))
    qb = q.reshape(bsz, n_kv, grp, nb, Q_BLOCK, dk).transpose(3, 0, 1, 2, 4, 5)

    def one_block(qblk):
        s = jnp.einsum('bkgqd,bksd->bkgqs', qblk, k).astype(jnp.float32) * scale
        p = jax.nn.softmax(s, axis=-1).astype(v.dtype)
        return jnp.einsum('bkgqs,bksd->bkgqd', p, v)

    out = lax.map(one_block, qb)
    out = out.transpose(1, 0, 4, 2, 3, 5)
    return out.reshape(bsz, s_len, n_heads * dv)

def setup_inputs(seed: int = 0) -> dict:
    key = jax.random.key(seed)
    ks = jax.random.split(key, 16)
    f32 = jnp.float32

    def w(k, shape, fan_in):
        return jax.random.normal(k, shape, f32) * (fan_in ** -0.5)

    def gain(k, shape):
        return 1.0 + 0.02 * jax.random.normal(k, shape, f32)

    return {
        "x": jax.random.normal(ks[0], (BATCH, SEQ, D_MODEL), f32),
        "norm_in": gain(ks[1], (DEPTH, D_MODEL)),
        "w_in": w(ks[2], (DEPTH, D_MODEL, N_IN), D_MODEL),
        "a_q_norm": gain(ks[3], (DEPTH, A_HEAD_DIM)),
        "a_k_norm": gain(ks[4], (DEPTH, A_HEAD_DIM)),
        "b_cq_norm": gain(ks[5], (DEPTH, B_Q_RANK)),
        "b_ckv_norm": gain(ks[6], (DEPTH, B_KV_RANK)),
        "w_uq": w(ks[7], (DEPTH, B_Q_RANK, B_HEADS * B_QK_DIM), B_Q_RANK),
        "w_ukv": w(ks[8], (DEPTH, B_KV_RANK, B_HEADS * (B_NOPE_DIM + B_V_HEAD_DIM)), B_KV_RANK),
        "b_q_norm": gain(ks[9], (DEPTH, B_QK_DIM)),
        "b_k_norm": gain(ks[10], (DEPTH, B_QK_DIM)),
        "w_out": w(ks[11], (DEPTH, D_MIX, D_MODEL), D_MIX),
    }

def reference(x, norm_in, w_in, a_q_norm, a_k_norm, b_cq_norm, b_ckv_norm,
              w_uq, w_ukv, b_q_norm, b_k_norm, w_out):
    bsz, s_len, _ = x.shape
    rope_a = axial_rope_tables(s_len, A_HEAD_DIM)
    rope_b = axial_rope_tables(s_len, B_ROPE_DIM)
    h = x
    for l in range(DEPTH):
        xn = rms_norm(h, norm_in[l])
        proj = jnp.einsum('bsd,dn->bsn', xn, w_in[l])
        a_q, a_k, a_v, a_g, b_cq, b_ckv, b_kr, b_g = jnp.split(proj, _SPLITS, axis=-1)

        q = a_q.reshape(bsz, s_len, A_HEADS, A_HEAD_DIM).transpose(0, 2, 1, 3)
        k = a_k.reshape(bsz, s_len, A_KV_HEADS, A_HEAD_DIM).transpose(0, 2, 1, 3)
        v = a_v.reshape(bsz, s_len, A_KV_HEADS, A_HEAD_DIM).transpose(0, 2, 1, 3)
        q = apply_axial_rope(rms_norm(q, a_q_norm[l]), rope_a)
        k = apply_axial_rope(rms_norm(k, a_k_norm[l]), rope_a)
        y_a = blocked_attention(q, k, v)

        c_q = rms_norm(b_cq, b_cq_norm[l])
        c_kv = rms_norm(b_ckv, b_ckv_norm[l])
        qb = jnp.einsum('bsr,rn->bsn', c_q, w_uq[l]).reshape(bsz, s_len, B_HEADS, B_QK_DIM)
        kvb = jnp.einsum('bsr,rn->bsn', c_kv, w_ukv[l]).reshape(
            bsz, s_len, B_HEADS, B_NOPE_DIM + B_V_HEAD_DIM)
        k_nope, vb = jnp.split(kvb, [B_NOPE_DIM], axis=-1)
        k_rope = jnp.broadcast_to(b_kr[:, :, None, :], (bsz, s_len, B_HEADS, B_ROPE_DIM))
        kb = jnp.concatenate([k_nope, k_rope], axis=-1)
        qb = rms_norm(qb, b_q_norm[l]).transpose(0, 2, 1, 3)
        kb = rms_norm(kb, b_k_norm[l]).transpose(0, 2, 1, 3)
        qb = jnp.concatenate([qb[..., :B_NOPE_DIM],
                              apply_axial_rope(qb[..., B_NOPE_DIM:], rope_b)], axis=-1)
        kb = jnp.concatenate([kb[..., :B_NOPE_DIM],
                              apply_axial_rope(kb[..., B_NOPE_DIM:], rope_b)], axis=-1)
        vb = vb.transpose(0, 2, 1, 3)
        y_b = blocked_attention(qb, kb, vb)

        y = jnp.concatenate([y_a * jax.nn.silu(a_g), y_b * jax.nn.silu(b_g)], axis=-1)
        h = h + jnp.einsum('bsm,md->bsd', y, w_out[l])
    return h


_drawn_inputs = setup_inputs


def setup_inputs(seed=0):
    import zlib

    import numpy as np

    out = dict(_drawn_inputs(seed))
    spreads = {}
    factors = {'norm_in': 8.0,
     'a_q_norm': 8.0,
     'a_k_norm': 8.0,
     'b_cq_norm': 8.0,
     'b_ckv_norm': 8.0,
     'b_q_norm': 8.0,
     'b_k_norm': 8.0}
    for name, (base, spread) in spreads.items():
        noise = np.random.default_rng([zlib.crc32(name.encode()), seed]).standard_normal(out[name].shape)
        drawn = base * np.exp(spread * noise) if base else spread * noise
        out[name] = __import__('jax').numpy.asarray(drawn.astype(out[name].dtype))
    for name, factor in factors.items():
        out[name] = (out[name] * factor).astype(out[name].dtype)
    return out
```

```python
from contextlib import ExitStack

import numpy as np
import concourse.bass as bass
from concourse import mybir

F32 = mybir.dt.float32
F16 = mybir.dt.float16
ALU = mybir.AluOpType
ACT = mybir.ActivationFunctionType
AX = mybir.AxisListType.X

P = 128
SEQ, D = 2048, 1024
EPS = 1e-6
GRID_W, THETA = 64, 10000.0
HA, GA, DA = 8, 2, 64
HB, NOPE, ROPE, DVB = 4, 64, 32, 128
DB = NOPE + ROPE
RQ, RKV = 384, 256
NIN = 2464
KT = D // P
TILES = SEQ // P
PAIRS = TILES // 2
QB = 512
NQ = SEQ // QB
QT = QB // P

CAK, CBQ, CBK, NZ = 512, 640, 1024, 1408
CHUNKS = [128 * c for c in range(5)] + [CBQ + DB * c for c in range(8)]
NZP = CHUNKS[-1] + P
NCH = len(CHUNKS)
PROJ = {"cq": (1280, 384), "ckv": (1664, 288), "aq": (0, 512), "akv": (512, 256), "ag": (768, 512), "bg": (1952, 512)}
PORDER = ["cq", "ckv", "aq", "akv", "ag", "bg"]


def rope_tables():
    rows = SEQ // GRID_W
    row = np.repeat(np.arange(rows, dtype=np.float32), GRID_W)
    col = np.tile(np.arange(GRID_W, dtype=np.float32), rows)
    out = []
    for dim in (DA, ROPE):
        half = dim // 2
        inv = (1.0 / (np.float32(THETA) ** (np.arange(0, half, 2, dtype=np.float32) / np.float32(half)))).astype(np.float32)
        ar, ac = row[:, None] * inv[None, :], col[:, None] * inv[None, :]
        out.append(np.concatenate([np.cos(ar), np.cos(ar), np.cos(ac), np.cos(ac)], 1))
        out.append(np.concatenate([-np.sin(ar), np.sin(ar), -np.sin(ac), np.sin(ac)], 1))
    return np.concatenate(out, 1).astype(np.float32)


def phase1(nc, x, w_in, w_uq, w_ukv, g_in, g_cq, g_ckv, g_heads, trig, eye, QA, KA, QBd, KBd, VA, VB, G):
    with ExitStack() as ctx:
        sb = lambda n, s, d=F32: ctx.enter_context(nc.sbuf_tensor("p1_" + n, s, d))
        ps = lambda n, s, d=F32: ctx.enter_context(nc.psum_tensor("p1_" + n, s, d))
        sem = lambda n: ctx.enter_context(nc.semaphore("p1_" + n))

        w_hi = sb("w_hi", [P, KT, NIN], F16)
        w_lo = sb("w_lo", [P, KT, NIN], F16)
        w_raw = sb("w_raw", [P, KT, 512])
        uq_hi = sb("uq_hi", [P, 3, HB * DB], F16)
        uq_lo = sb("uq_lo", [P, 3, HB * DB], F16)
        ukv_hi = sb("ukv_hi", [P, 2, HB * (NOPE + DVB)], F16)
        ukv_lo = sb("ukv_lo", [P, 2, HB * (NOPE + DVB)], F16)
        gin = sb("gin", [P, KT])
        gcq = sb("gcq", [P, 3])
        gckv = sb("gckv", [P, 2])
        gains = sb("gains", [P, NZ])
        eye32 = sb("eye32", [P, P])
        ident = sb("ident", [P, P], F16)
        eps = sb("eps", [P, 1])
        xin = sb("xin", [P, 2, D])
        trg = sb("trg", [P, 2, 192])
        stat = sb("stat", [P, 2, 8])
        lstat = sb("lstat", [P, 2, 8])
        xh = sb("xh", [P, D], F16)
        xl = sb("xl", [P, D], F16)
        junk = sb("junk", [P, NZ])
        xT = sb("xT", [P, 2, 2, KT, P], F16)
        cq32 = sb("cq32", [P, RQ])
        ckv32 = sb("ckv32", [P, RKV + ROPE])
        lat_hi = sb("lat_hi", [P, RQ + RKV], F16)
        lat_lo = sb("lat_lo", [P, RQ + RKV], F16)
        latT = sb("latT", [P, 10, P], F16)
        R = sb("R", [P, 2, NZ])
        sq = sb("sq", [P, NZ])
        rstat = sb("rstat", [P, 3, 18])
        T2 = sb("T2", [P, CBQ + 8 * ROPE])
        zh = sb("zh", [P, NZP], F16)
        zl = sb("zl", [P, NZP], F16)
        zT = sb("zT", [P, 2 * NCH, 2 * P], F16)
        va32 = sb("va32", [P, GA * DA])
        vb32 = sb("vb32", [P, HB, DVB])
        va = sb("va", [P, GA, 2 * DA + 1], F16)
        vb = sb("vb", [P, HB, 2 * DVB + 1], F16)
        g32 = sb("g32", [P, D])

        ring = [ps(f"ring{i}", [P, 512]) for i in range(3)]
        xtp = [ps(f"xtp{i}", [P, KT, P], F16) for i in range(2)]
        trp = [ps(f"trp{i}", [P, KT, P], F16) for i in range(3)]

        s_const = sem("const_loaded")
        s_x = [sem("x_loaded0"), sem("x_loaded1")]
        s_trig = [sem("trig_loaded0"), sem("trig_loaded1")]
        s_w = sem("w_loaded")
        s_whi = sem("w_hi_split")
        s_wlo = sem("w_lo_split")
        s_ident = sem("ident_ready")
        s_eps = sem("eps_ready")
        s_ones = sem("ones_ready")
        s_ax = sem("act_x_chain")
        s_dx = sem("dve_x")
        s_xtp = sem("xT_in_psum")
        s_xt = sem("xT_in_sbuf")
        s_proj = sem("proj_done")
        s_ring = sem("ring_read")
        s_lat = sem("act_latents")
        s_dlat = sem("dve_latents")
        s_ltp = sem("latT_in_psum")
        s_lt = sem("latT_in_sbuf")
        s_R = sem("R_written")
        s_sq = sem("R_squared")
        s_hsum = sem("head_sums")
        s_hdev = sem("head_deviations")
        s_rc = sem("rope_chain")
        s_zh = sem("z_hi")
        s_zl = sem("z_lo")
        s_zp = sem("zT_in_psum")
        s_zt = sem("zT_in_sbuf")
        s_zst = sem("zT_stored")
        s_v32 = sem("v_raw")
        s_vhi = sem("v_hi")
        s_vlo = sem("v_lo")
        s_vst = sem("v_stored")
        s_gst = sem("gate_stored")
        RC = 6
        ZST = 12 * 16
        ZG = [(0, 7), (7, 13), (13, 20), (20, 26)]

        xt = x.rearrange("b (t p) d -> (b t) p d", p=P)
        trt = trig.rearrange("(t p) c -> t p c", p=P)
        w3 = w_in.rearrange("l (k p) n -> (l p) k n", p=P)

        def loop(eng, body):
            body(0, True, False)
            with eng.Fori(1, PAIRS - 1) as i:
                body(i, False, False)
            body(PAIRS - 1, False, True)

        block = ctx.enter_context(nc.Block())

        @block.sync
        def _(sp):
            sp.dma_start(xin[:, 0, :], xt[0]).then_inc(s_x[0], 16)
            sp.dma_start(gin[:, :], g_in.rearrange("l (k p) -> (l p) k", p=P), allow_slow_non_contiguous=True).then_inc(s_const, 16)
            sp.dma_start(eye32[:, :], eye).then_inc(s_const, 16)
            sp.dma_start(gcq[:, :], g_cq.rearrange("l (k p) -> (l p) k", p=P), allow_slow_non_contiguous=True).then_inc(s_const, 16)
            sp.dma_start(gckv[:, :], g_ckv.rearrange("l (k p) -> (l p) k", p=P), allow_slow_non_contiguous=True).then_inc(s_const, 16)
            sp.dma_start(gains[:, :], g_heads.partition_broadcast(P)).then_inc(s_const, 16)
            for n, name in enumerate(PORDER):
                c0, w = PROJ[name]
                if n:
                    sp.wait_ge(s_whi, n)
                    sp.wait_ge(s_wlo, n)
                sp.dma_start(w_raw[:, :, 0:w], w3[:, :, c0:c0 + w]).then_inc(s_w, 16)
                if n == 0:
                    sp.dma_start(xin[:, 1, :], xt[1]).then_inc(s_x[1], 16)
                    sp.dma_start(trg[:, 0, :], trt[0]).then_inc(s_trig[0], 16)
            sp.wait_ge(s_whi, 6)
            sp.wait_ge(s_wlo, 6)
            sp.dma_start(w_raw[:, 0:3, 0:HB * DB], w_uq.rearrange("l (k p) n -> (l p) k n", p=P)).then_inc(s_w, 16)
            sp.wait_ge(s_whi, 7)
            sp.wait_ge(s_wlo, 7)
            ukv_raw = w_raw[:, 0:3, :].rearrange("p k n -> p (k n)").rearrange("p (k n) -> p k n", n=768)
            sp.dma_start(ukv_raw, w_ukv.rearrange("l (k p) n -> (l p) k n", p=P)).then_inc(s_w, 16)

            def tile(i, h, first, last):
                t = i * 2 + h
                if not (last and h == 1):
                    if not (first and h == 0):
                        sp.wait_ge(s_rc, t * RC)
                    sp.dma_start(trg[:, 1 - h, :], trt[t + 1]).then_inc(s_trig[1 - h], 16)
                if not last:
                    sp.wait_ge(s_dx, t * 2 + 2)
                    sp.dma_start(xin[:, h, :], xt[t + 2]).then_inc(s_x[h], 16)
                if h == 0 and not first:
                    sp.wait_ge(s_zt, t * 4)
                    store_z(i - 1)
                sp.wait_ge(s_vhi, t + 1)
                sp.wait_ge(s_vlo, t + 1)
                sp.dma_start(VA[t], va[:, :, :]).then_inc(s_vst, 16)
                sp.dma_start(VB[t], vb[:, :, :]).then_inc(s_vst, 16)
                sp.wait_ge(s_ring, t * 9 + 9)
                sp.dma_start(G[t], g32[:, :]).then_inc(s_gst, 16)

            def store_z(pr):
                for s in range(2):
                    for h2 in range(2):
                        rows = slice(64 * h2, 64 * h2 + 64)
                        sp.dma_start(QA[s].rearrange("(c h) pr r t -> h pr r c t", h=2)[h2, pr],
                                     zT[rows, NCH * s:NCH * s + 4, :]).then_inc(s_zst, 16)
                        sp.dma_start(KA[s, h2, pr], zT[rows, NCH * s + 4, :]).then_inc(s_zst, 16)
                    sp.dma_start(QBd[s].rearrange("h pr r t -> pr r h t")[pr],
                                 zT[0:DB, NCH * s + 5:NCH * s + 9, :]).then_inc(s_zst, 16)
                    sp.dma_start(KBd[s].rearrange("h pr r t -> pr r h t")[pr],
                                 zT[0:DB, NCH * s + 9:NCH * s + 13, :]).then_inc(s_zst, 16)

            loop(sp, lambda i, first, last: [tile(i, h, first, last) for h in range(2)])
            sp.wait_ge(s_zt, TILES * 4)
            store_z(PAIRS - 1)
            sp.wait_ge(s_zst, PAIRS * ZST)
            sp.wait_ge(s_vst, TILES * 32)
            sp.wait_ge(s_gst, TILES * 16)

        @block.gpsimd
        def _(pool):
            pool.memset(va[:, :, 2 * DA:2 * DA + 1], 1.0).then_inc(s_ones, 1)
            pool.memset(vb[:, :, 2 * DVB:2 * DVB + 1], 1.0).then_inc(s_ones, 1)
            pool.memset(zh[:, NZ:], 0.0).then_inc(s_ones, 1)
            pool.memset(zl[:, NZ:], 0.0).then_inc(s_ones, 1)

        @block.scalar
        def _(act):
            def x_hi(t, h):
                st = stat[:, h, :]
                act.wait_ge(s_x[h], x_count(t, h))
                act.activation(junk[:, 0:D], xin[:, h, :], ACT.Square, accum_out=st[:, 0:1]).then_inc(s_ax, 1)
                act.wait_ge(s_ax, t * 3 + 1)
                act.activation(st[:, 1:2], st[:, 0:1], ACT.Sqrt, bias=eps[:, :], scale=1.0 / D).then_inc(s_ax, 1)
                act.wait_ge(s_dx, t * 2 + 1)
                if not zero(t):
                    act.wait_ge(s_xtp, t * 2)
                act.activation(xh[:, :], xin[:, h, :], ACT.Copy, scale=st[:, 2:3]).then_inc(s_ax, 1)

            def evac(t, n, *pairs):
                act.wait_ge(s_proj, t * 9 + n + 1)
                for dst, src in pairs:
                    last = act.activation(dst, src, ACT.Copy)
                last.then_inc(s_ring, 1)

            def z_hi(t, h):
                act.wait_ge(s_rc, t * RC + RC)
                if not zero(t):
                    act.wait_ge(s_zp, t * 4)
                act.activation(zh[:, 0:NZ], R[:, h, :], ACT.Copy).then_inc(s_zh, 1)

            def z_evac(t, h, pair):
                for n, (a, b) in enumerate(ZG):
                    act.wait_ge(s_zp, t * 4 + n + 1)
                    if n == 0 and h == 0 and pair is not None:
                        act.wait_ge(s_zst, pair * ZST)
                    act.activation(zT[:, a:b, P * h:P * h + P], trp[n % 3][:, 0:b - a, :], ACT.Copy).then_inc(s_zt, 1)

            def tile(i, h, first, last):
                t = i * 2 + h
                Rh = R[:, h, :]
                if not (last and h == 1):
                    x_hi(t + 1, 1 - h)
                if not (first and h == 0):
                    z_hi(t - 1, 1 - h)
                ls = lstat[:, h, :]
                if not (first and h == 0):
                    act.wait_ge(s_dlat, t * 2)
                evac(t, 0, (cq32[:, :], ring[0][:, 0:RQ]))
                evac(t, 1, (ckv32[:, :], ring[1][:, 0:RKV + ROPE]))
                act.wait_ge(s_ring, t * 9 + 2)
                act.activation(junk[:, 0:RQ], cq32[:, :], ACT.Square, accum_out=ls[:, 0:1]).then_inc(s_lat, 1)
                act.activation(junk[:, RQ:RQ + RKV], ckv32[:, 0:RKV], ACT.Square, accum_out=ls[:, 1:2]).then_inc(s_lat, 1)
                act.wait_ge(s_lat, t * 5 + 2)
                act.activation(ls[:, 2:3], ls[:, 0:1], ACT.Sqrt, bias=eps[:, :], scale=1.0 / RQ).then_inc(s_lat, 1)
                act.activation(ls[:, 3:4], ls[:, 1:2], ACT.Sqrt, bias=eps[:, :], scale=1.0 / RKV).then_inc(s_lat, 1)
                evac(t, 2, (Rh[:, 0:512], ring[2][:, :]))
                act.wait_ge(s_dlat, t * 2 + 1)
                if not (first and h == 0):
                    act.wait_ge(s_ltp, t * 2)
                act.activation(lat_hi[:, 0:RQ], cq32[:, :], ACT.Copy, scale=ls[:, 4:5])
                act.activation(lat_hi[:, RQ:], ckv32[:, 0:RKV], ACT.Copy, scale=ls[:, 5:6]).then_inc(s_lat, 1)
                if not (first and h == 0):
                    act.wait_ge(s_vlo, t)
                evac(t, 3, (Rh[:, CAK:CBQ], ring[0][:, 0:128]), (va32[:, :], ring[0][:, 128:256]))
                if not (first and h == 0):
                    act.wait_ge(s_gst, t * 16)
                evac(t, 4, (g32[:, 0:512], ring[1][:, :]))
                kb = Rh[:, CBK:NZ].rearrange("p (h d) -> p h d", d=DB)
                act.activation(kb[:, :, NOPE:DB], ckv32[:, RKV:RKV + ROPE].unsqueeze(1).to_broadcast([P, HB, ROPE]), ACT.Copy)
                evac(t, 5, (Rh[:, CBQ:CBK], ring[2][:, 0:384]))
                for n in range(2):
                    r = ring[n][:, 0:384].rearrange("p (h d) -> p h d", d=NOPE + DVB)
                    evac(t, 6 + n, (vb32[:, 2 * n:2 * n + 2, :], r[:, :, NOPE:]), (kb[:, 2 * n:2 * n + 2, 0:NOPE], r[:, :, 0:NOPE]))
                act.wait_ge(s_ring, t * 9 + 8)
                if not (first and h == 0):
                    act.wait_ge(s_hsum, t * 2)
                act.activation(sq[:, :], Rh, ACT.Square).then_inc(s_sq, 1)
                if first and h == 0:
                    act.wait_ge(s_ones, 2)
                else:
                    act.wait_ge(s_vst, t * 32)
                act.activation(va[:, :, DA:2 * DA], va32[:, :].rearrange("p (g d) -> p g d", d=DA), ACT.Copy)
                act.activation(vb[:, :, DVB:2 * DVB], vb32[:, :, :], ACT.Copy).then_inc(s_vhi, 1)
                if not (first and h == 0):
                    z_evac(t - 1, 1 - h, None if (first or (h == 1 and first)) else (i if h == 1 else None))
                act.wait_ge(s_hsum, t * 2 + 2)
                act.activation(rstat[:, 1, 0:10], rstat[:, 0, 0:10], ACT.Sqrt, bias=eps[:, :], scale=1.0 / DA)
                act.activation(rstat[:, 1, 10:18], rstat[:, 0, 10:18], ACT.Sqrt, bias=eps[:, :], scale=1.0 / DB).then_inc(s_hdev, 1)
                act.wait_ge(s_proj, t * 9 + 9)
                act.activation(g32[:, 512:], ring[2][:, :], ACT.Copy).then_inc(s_ring, 1)

            act.wait_ge(s_const, 80)
            act.activation(ident[:, :], eye32[:, :], ACT.Copy).then_inc(s_ident, 1)
            act.wait_ge(s_eps, 1)
            x_hi(0, 0)
            for n, name in enumerate(PORDER):
                c0, w = PROJ[name]
                act.wait_ge(s_w, 16 * n + 16)
                for k in range(KT):
                    last = act.activation(w_hi[:, k, c0:c0 + w], w_raw[:, k, 0:w], ACT.Copy, scale=gin[:, k:k + 1])
                last.then_inc(s_whi, 1)
            act.wait_ge(s_w, 112)
            for k in range(3):
                last = act.activation(uq_hi[:, k, :], w_raw[:, k, 0:HB * DB], ACT.Copy, scale=gcq[:, k:k + 1])
            last.then_inc(s_whi, 1)
            act.wait_ge(s_w, 128)
            ukv_raw = w_raw[:, 0:3, :].rearrange("p k n -> p (k n)").rearrange("p (k n) -> p k n", n=768)
            for k in range(2):
                last = act.activation(ukv_hi[:, k, :], ukv_raw[:, k, :], ACT.Copy, scale=gckv[:, k:k + 1])
            last.then_inc(s_whi, 1)
            loop(act, lambda i, first, last: [tile(i, h, first, last) for h in range(2)])
            z_hi(TILES - 1, 1)
            z_evac(TILES - 1, 1, None)

        @block.vector
        def _(dve):
            def x_rstd(t, h):
                dve.wait_ge(s_ax, t * 3 + 2)
                dve.reciprocal(stat[:, h, 2:3], stat[:, h, 1:2]).then_inc(s_dx, 1)

            def x_lo(t, h):
                dve.wait_ge(s_dx, t * 2 + 1)
                dve.wait_ge(s_ax, t * 3 + 3)
                if not zero(t):
                    dve.wait_ge(s_xtp, t * 2)
                dve.scalar_tensor_tensor(out=xl[:, :], in0=xin[:, h, :], scalar=stat[:, h, 2:3], in1=xh[:, :],
                                         op0=ALU.mult, op1=ALU.subtract).then_inc(s_dx, 1)

            def xt_evac(t, h):
                for s in range(2):
                    dve.wait_ge(s_xtp, t * 2 + s + 1)
                    dve.tensor_copy(xT[:, h, s], xtp[s][:, :, :]).then_inc(s_xt, 1)

            def z_lo(t, h):
                dve.wait_ge(s_zh, t + 1)
                if not zero(t):
                    dve.wait_ge(s_zp, t * 4)
                dve.tensor_tensor(zl[:, 0:NZ], R[:, h, :], zh[:, 0:NZ], ALU.subtract).then_inc(s_zl, 1)

            def tile(i, h, first, last):
                t = i * 2 + h
                Rh = R[:, h, :]
                if not (last and h == 1):
                    x_rstd(t + 1, 1 - h)
                if not (first and h == 0):
                    z_lo(t - 1, 1 - h)
                if not (last and h == 1):
                    x_lo(t + 1, 1 - h)
                ls = lstat[:, h, :]
                dve.wait_ge(s_lat, t * 5 + 4)
                dve.reciprocal(ls[:, 4:6], ls[:, 2:4]).then_inc(s_dlat, 1)
                dve.wait_ge(s_dlat, t * 2 + 1)
                dve.wait_ge(s_lat, t * 5 + 5)
                dve.scalar_tensor_tensor(out=lat_lo[:, 0:RQ], in0=cq32[:, :], scalar=ls[:, 4:5], in1=lat_hi[:, 0:RQ],
                                         op0=ALU.mult, op1=ALU.subtract)
                dve.scalar_tensor_tensor(out=lat_lo[:, RQ:], in0=ckv32[:, 0:RKV], scalar=ls[:, 5:6], in1=lat_hi[:, RQ:],
                                         op0=ALU.mult, op1=ALU.subtract).then_inc(s_dlat, 1)
                dve.wait_ge(s_ltp, t * 2 + 1)
                dve.tensor_copy(latT[:, 0:6, :], trp[0][:, 0:6, :])
                dve.wait_ge(s_ltp, t * 2 + 2)
                dve.tensor_copy(latT[:, 6:10, :], trp[1][:, 0:4, :]).then_inc(s_lt, 1)
                if not (last and h == 1):
                    xt_evac(t + 1, 1 - h)
                dve.wait_ge(s_sq, t + 1)
                if not (first and h == 0):
                    dve.wait_ge(s_hdev, t)
                dve.tensor_reduce(rstat[:, 0, 0:10], sq[:, 0:CBQ].rearrange("p (h d) -> p h d", d=DA), AX, ALU.add).then_inc(s_hsum, 1)
                dve.tensor_reduce(rstat[:, 0, 10:18], sq[:, CBQ:].rearrange("p (h d) -> p h d", d=DB), AX, ALU.add).then_inc(s_hsum, 1)
                dve.wait_ge(s_vhi, t + 1)
                dve.tensor_tensor(va[:, :, 0:DA], va32[:, :].rearrange("p (g d) -> p g d", d=DA), va[:, :, DA:2 * DA], ALU.subtract)
                dve.tensor_tensor(vb[:, :, 0:DVB], vb32[:, :, :], vb[:, :, DVB:2 * DVB], ALU.subtract).then_inc(s_vlo, 1)
                dve.wait_ge(s_hdev, t + 1)
                dve.reciprocal(rstat[:, 2, :], rstat[:, 1, :]).then_inc(s_rc, 1)
                dve.wait_ge(s_rc, t * RC + 1)
                ra = Rh[:, 0:CBQ].rearrange("p (h d) -> p h d", d=DA)
                rb = Rh[:, CBQ:].rearrange("p (h d) -> p h d", d=DB)
                dve.tensor_tensor(ra, ra, rstat[:, 2, 0:10].unsqueeze(2).to_broadcast([P, 10, DA]), ALU.mult)
                dve.tensor_tensor(rb, rb, rstat[:, 2, 10:18].unsqueeze(2).to_broadcast([P, 8, DB]), ALU.mult).then_inc(s_rc, 1)
                dve.wait_ge(s_rc, t * RC + 2)
                dve.tensor_tensor(Rh, Rh, gains[:, :], ALU.mult).then_inc(s_rc, 1)
                dve.wait_ge(s_rc, t * RC + 3)
                dve.wait_ge(s_trig[h], i * 16 + 16)
                tr = trg[:, h, :]
                parts = ((ra, T2[:, 0:CBQ].rearrange("p (h d) -> p h d", d=DA), 10, 0, 64),
                         (rb[:, :, NOPE:], T2[:, CBQ:].rearrange("p (h d) -> p h d", d=ROPE), 8, 128, 32))
                for r, t2, nh, c0, w in parts:
                    c = w // 4
                    rv = r.rearrange("p h (a f c) -> p h a f c", a=2, f=2)
                    tv = t2.rearrange("p h (a f c) -> p h a f c", a=2, f=2)
                    sv = tr[:, c0 + w:c0 + 2 * w].rearrange("p (a f c) -> p a f c", a=2, f=2)
                    for f in range(2):
                        last_op = dve.tensor_tensor(tv[:, :, :, f, :], rv[:, :, :, 1 - f, :],
                                                    sv[:, :, f, :].unsqueeze(1).to_broadcast([P, nh, 2, c]), ALU.mult)
                last_op.then_inc(s_rc, 1)
                dve.wait_ge(s_rc, t * RC + 4)
                for r, t2, nh, c0, w in parts:
                    last_op = dve.tensor_tensor(r, r, tr[:, c0:c0 + w].unsqueeze(1).to_broadcast([P, nh, w]), ALU.mult)
                last_op.then_inc(s_rc, 1)
                dve.wait_ge(s_rc, t * RC + 5)
                for r, t2, nh, c0, w in parts:
                    last_op = dve.tensor_tensor(r, r, t2, ALU.add)
                last_op.then_inc(s_rc, 1)

            dve.memset(eps[:, :], EPS).then_inc(s_eps, 1)
            x_rstd(0, 0)
            x_lo(0, 0)
            xt_evac(0, 0)

            def split_lo(n, pieces):
                dve.wait_ge(s_whi, n + 1)
                for lo, raw, g, hi in pieces:
                    last = dve.scalar_tensor_tensor(out=lo, in0=raw, scalar=g, in1=hi, op0=ALU.mult, op1=ALU.subtract)
                last.then_inc(s_wlo, 1)

            dve.wait_ge(s_const, 80)
            for n, name in enumerate(PORDER):
                c0, w = PROJ[name]
                split_lo(n, [(w_lo[:, k, c0:c0 + w], w_raw[:, k, 0:w], gin[:, k:k + 1], w_hi[:, k, c0:c0 + w]) for k in range(KT)])
            split_lo(6, [(uq_lo[:, k, :], w_raw[:, k, 0:HB * DB], gcq[:, k:k + 1], uq_hi[:, k, :]) for k in range(3)])
            ukv_raw = w_raw[:, 0:3, :].rearrange("p k n -> p (k n)").rearrange("p (k n) -> p k n", n=768)
            split_lo(7, [(ukv_lo[:, k, :], ukv_raw[:, k, :], gckv[:, k:k + 1], ukv_hi[:, k, :]) for k in range(2)])
            loop(dve, lambda i, first, last: [tile(i, h, first, last) for h in range(2)])
            z_lo(TILES - 1, 1)

        @block.tensor
        def _(pe):
            def project(t, n, w, terms, new):
                if not (new and n < 3):
                    pe.wait_ge(s_ring, t * 9 + n - 2)
                for m, (a, b) in enumerate(terms):
                    last = pe.matmul(ring[n % 3][:, 0:w], a, b, start=(m == 0), stop=(m == len(terms) - 1))
                last.then_inc(s_proj, 1)

            def proj_in(t, h, name, n, new):
                c0, w = PROJ[name]
                if new:
                    pe.wait_ge(s_whi, PORDER.index(name) + 1)
                    pe.wait_ge(s_wlo, PORDER.index(name) + 1)
                cols = slice(c0, c0 + w)
                terms = []
                for k in range(KT):
                    terms += [(xT[:, h, 0, k, :], w_hi[:, k, cols]), (xT[:, h, 0, k, :], w_lo[:, k, cols]),
                              (xT[:, h, 1, k, :], w_hi[:, k, cols])]
                project(t, n, w, terms, new)

            def transpose_x(t, h):
                for s, src in enumerate((xh, xl)):
                    if s == 0:
                        pe.wait_ge(s_ax, t * 3 + 3)
                    else:
                        pe.wait_ge(s_dx, t * 2 + 2)
                    if not zero(t):
                        pe.wait_ge(s_xt, t * 2 - 1 + s)
                    for k in range(KT):
                        last = pe.transpose(xtp[s][:, k, :], src[:, k * P:(k + 1) * P], ident[:, :])
                    last.then_inc(s_xtp, 1)

            def transpose_latents(t, new):
                pe.wait_ge(s_lat, t * 5 + 5)
                pe.wait_ge(s_dlat, t * 2 + 2)
                if not new:
                    pe.wait_ge(s_lt, t)
                for b, (c0, nk) in enumerate(((0, 3), (RQ, 2))):
                    for s, src in enumerate((lat_hi, lat_lo)):
                        for k in range(nk):
                            last = pe.transpose(trp[b][:, s * nk + k, :], src[:, c0 + k * P:c0 + (k + 1) * P], ident[:, :])
                    last.then_inc(s_ltp, 1)

            def transpose_z(t, after):
                pe.wait_ge(s_zh, t + 1)
                if after is not None:
                    pe.wait_ge(s_lt, after)
                for n, (a, b) in enumerate(ZG):
                    if n == 2:
                        pe.wait_ge(s_zl, t + 1)
                    if n == 3:
                        pe.wait_ge(s_zt, t * 4 + 1)
                    for j in range(a, b):
                        c0 = CHUNKS[j % NCH]
                        src = zh if j < NCH else zl
                        last = pe.transpose(trp[n % 3][:, j - a, :], src[:, c0:c0 + P], ident[:, :])
                    last.then_inc(s_zp, 1)

            def tile(i, h, first, last):
                t = i * 2 + h
                new = first and h == 0
                pe.wait_ge(s_xt, t * 2 + 2)
                proj_in(t, h, "cq", 0, new)
                proj_in(t, h, "ckv", 1, new)
                proj_in(t, h, "aq", 2, new)
                if not new:
                    if not (first and h == 1):
                        pe.wait_ge(s_zt, t * 4 - 4)
                transpose_latents(t, new)
                proj_in(t, h, "akv", 3, new)
                proj_in(t, h, "ag", 4, new)
                pe.wait_ge(s_lt, t + 1)
                if new:
                    pe.wait_ge(s_whi, 8)
                    pe.wait_ge(s_wlo, 8)
                terms = []
                for k in range(3):
                    terms += [(latT[:, k, :], uq_hi[:, k, :]), (latT[:, k, :], uq_lo[:, k, :]), (latT[:, 3 + k, :], uq_hi[:, k, :])]
                project(t, 5, 384, terms, new)
                for n in range(2):
                    cols = slice(384 * n, 384 * n + 384)
                    terms = []
                    for k in range(2):
                        terms += [(latT[:, 6 + k, :], ukv_hi[:, k, cols]), (latT[:, 6 + k, :], ukv_lo[:, k, cols]),
                                  (latT[:, 8 + k, :], ukv_hi[:, k, cols])]
                    project(t, 6 + n, 384, terms, new)
                if not new:
                    transpose_z(t - 1, t + 1)
                if not (last and h == 1):
                    transpose_x(t + 1, 1 - h)
                proj_in(t, h, "bg", 8, new)

            pe.wait_ge(s_ident, 1)
            pe.wait_ge(s_ones, 4)
            transpose_x(0, 0)
            loop(pe, lambda i, first, last: [tile(i, h, first, last) for h in range(2)])
            transpose_z(TILES - 1, None)


def zero(t):
    return isinstance(t, int) and t == 0


def x_count(t, h):
    return (t - h) * 8 + 16


def phase2(nc, QA, KA, QBd, KBd, VA, VB, YA, YB):
    LEAD = 12
    STEPS = 8
    HALF = 3 * STEPS
    N = SEQ // QB * HB
    N32, NP = 3, 6
    KW = 2 * QB
    ONE = 64.0
    with ExitStack() as ctx:
        sb = lambda n, s, d=F32: ctx.enter_context(nc.sbuf_tensor("p2_" + n, s, d))
        ps = lambda n, s, d=F32: ctx.enter_context(nc.psum_tensor("p2_" + n, s, d))
        sem = lambda n: ctx.enter_context(nc.semaphore("p2_" + n))

        ka_hl = [sb(f"ka_hl{g}", [P, SEQ], F16) for g in range(GA)]
        ka_h1 = [sb(f"ka_h1{g}", [66, SEQ], F16) for g in range(GA)]
        vas = sb("vas", [P, TILES, GA, 2 * DA + 1], F16)
        kb_h1 = sb("kb_h1", [DB + 2, SEQ], F16)
        kb_l = sb("kb_l", [DB, SEQ], F16)
        vbs = sb("vbs", [P, TILES, 2 * DVB + 1], F16)
        qa_hh = [sb(f"qa_hh{g}", [P, QB], F16) for g in range(GA)]
        qa_lm = [sb(f"qa_lm{g}", [66, QB], F16) for g in range(GA)]
        qb_h = sb("qb_h", [DB, QB], F16)
        qb_lm = sb("qb_lm", [DB + 2, QB], F16)
        p32 = sb("p32", [P, N32, KW])
        ph = sb("ph", [P, NP, 2, QB], F16)
        pl = sb("pl", [P, NP, 2, QB], F16)
        part = sb("part", [P, 2, 8])
        rowmax = sb("rowmax", [P, 2, QT])
        mpair = sb("mpair", [P, 2, QT, 2], F16)
        eye = sb("eye", [P, P], F16)
        acc_sb = sb("acc_sb", [P, QT, 2 * DA + 1])
        rden = sb("rden", [P, QT])
        ysum = sb("ysum", [P, QT, DVB])
        yout = sb("yout", [P, 2, QT, DVB])

        mx = ps("mx", [P, 2, QB])
        st = ps("st", [P, 2, 2, QB])
        acc = ps("acc", [P, 2, 512])
        accv = acc[:, :, 0:258].rearrange("p b (j c) -> p b j c", j=2)

        s_ka = sem("ka_loaded")
        s_va = sem("va_loaded")
        s_q = [sem(f"q_loaded{p}") for p in range(3)]
        s_kb = sem("kb_loaded")
        s_vb = sem("vb_loaded")
        s_const = sem("constants")
        s_eye = sem("eye_ready")
        s_mx = sem("max_scores")
        s_red = sem("max_reduced")
        s_md = sem("max_chain")
        s_mt = sem("max_turned")
        s_mr = sem("max_rows")
        s_st = sem("scores")
        s_exp = sem("exp_done")
        s_hi = sem("p_hi")
        s_lo = sem("p_lo")
        s_pv = sem("pv_done")
        s_acc = sem("acc_copied")
        s_rden = sem("rden")
        s_y = sem("y_chain")
        s_yst = sem("y_stored")

        UNITS = [(0, "a"), (1, "a"), (0, "b")]

        def y_before(i, pos):
            return i * 5 + 2 * pos

        def before(i, s, act_on, first):
            pos = s // STEPS - 1
            act_on(i if pos >= 0 else i - 1, pos % 3, first and pos == 0)

        def loop(eng, body):
            body(0, True, False)
            with eng.Fori(1, N - 1) as i:
                body(i, False, False)
            body(N - 1, False, True)

        block = ctx.enter_context(nc.Block())

        @block.sync
        def _(sp):
            def load_q(i, pos):
                g, kind = UNITS[pos]
                if kind == "a":
                    for s, dsts in ((0, (qa_hh[g][0:64, :], qa_hh[g][64:128, :])), (1, (qa_lm[g][0:64, :],))):
                        src = QA[s].rearrange("(g h) (q two) r t -> g (h q) r two t", g=GA, two=2)[g, i]
                        for dst in dsts:
                            sp.dma_start(dst.rearrange("r (two t) -> r two t", two=2), src).then_inc(s_q[pos], 16)
                else:
                    for s, dst in enumerate((qb_h[:, :], qb_lm[0:DB, :])):
                        src = QBd[s].rearrange("h (q two) r t -> (h q) r two t", two=2)[i]
                        sp.dma_start(dst.rearrange("r (two t) -> r two t", two=2), src).then_inc(s_q[pos], 16)

            def load_kb(h):
                for s, dst in enumerate((kb_h1[0:DB, :], kb_l[:, :])):
                    sp.dma_start(dst.rearrange("r (pr t) -> r pr t", pr=PAIRS),
                                 KBd[s, h].rearrange("pr r t -> r pr t")).then_inc(s_kb, 16)

            def load_vb(h):
                sp.dma_start(vbs[:, :, :], VB.rearrange("t p h c -> h p t c")[h]).then_inc(s_vb, 16)

            def store_y(i, pos):
                sp.wait_ge(s_y, y_before(i, pos) + (2 if pos < 2 else 1))
                g, kind = UNITS[pos]
                if kind == "a":
                    sp.dma_start(YA[g].rearrange("h (q j) p d -> (h q) p j d", j=QT)[i], yout[:, pos % 2, :, 0:DA]).then_inc(s_yst, 16)
                else:
                    sp.dma_start(YB.rearrange("h (q j) p d -> (h q) p j d", j=QT)[i], yout[:, pos % 2, :, :]).then_inc(s_yst, 16)

            for g in range(GA):
                for s, dsts in ((0, (ka_hl[g][0:64, :], ka_h1[g][0:64, :])), (1, (ka_hl[g][64:128, :],))):
                    for dst in dsts:
                        sp.dma_start(dst.rearrange("r (pr t) -> r pr t", pr=PAIRS),
                                     KA[s, g].rearrange("pr r t -> r pr t")).then_inc(s_ka, 16)
                load_q(0, g)
            load_kb(0)
            load_q(0, 2)
            sp.dma_start(vas[:, :, :, :], VA.rearrange("t p g c -> p t g c")).then_inc(s_va, 16)
            load_vb(0)

            def body(i, h):
                for pos in range(3):
                    sp.wait_ge(s_st, i * HALF + (pos + 1) * STEPS)
                    load_q(i + 1, pos)
                    if pos < 2:
                        store_y(i, pos)
                load_kb(h)
                sp.wait_ge(s_pv, i * HALF + HALF)
                load_vb(h)
                store_y(i, 2)

            for h in range(HB):
                with sp.Fori(max(h * NQ - 1, 0), h * NQ + NQ - 1) as i:
                    body(i, h)
            for pos in range(3):
                store_y(N - 1, pos)
            sp.wait_ge(s_yst, N * 48)

        @block.gpsimd
        def _(pool):
            pool.memset(eye[:, :], 0.0).then_inc(s_eye, 1)
            pool.wait_ge(s_eye, 1)
            pool.affine_select(out=eye[:, :], in_=eye[:, :], compare_op=ALU.not_equal, fill=1.0,
                               base=0, pattern=[[-1, P]], channel_multiplier=1).then_inc(s_eye, 1)

            def unit(i, pos, first):
                u = i * 3 + pos
                kind = UNITS[pos][1]
                w = DA if kind == "a" else DVB
                if kind == "a":
                    pool.wait_ge(s_acc, u + 1)
                    pool.tensor_tensor(ysum[:, :, 0:w], acc_sb[:, :, 0:DA], acc_sb[:, :, DA:2 * DA], ALU.add).then_inc(s_y, 1)
                    src = ysum[:, :, 0:w]
                    pool.wait_ge(s_y, y_before(i, pos) + 1)
                else:
                    pool.wait_ge(s_acc, u + 1)
                    src = acc_sb[:, :, 0:w]
                pool.wait_ge(s_rden, u + 1)
                if not (first and pos == 0):
                    pool.wait_ge(s_yst, u * 16)
                pool.tensor_tensor(yout[:, pos % 2, :, 0:w], src, rden[:, :].unsqueeze(2).to_broadcast([P, QT, w]),
                                   ALU.mult).then_inc(s_y, 1)

            loop(pool, lambda i, first, last: [unit(i, pos, first) for pos in range(3)])

        @block.scalar
        def _(act):
            def copy_acc(i, pos, first):
                act.wait_ge(s_pv, i * HALF + pos * STEPS + STEPS)
                if not first:
                    act.wait_ge(s_y, y_before(i, pos))
                act.activation(acc_sb[:, :, :].rearrange("p (b j) c -> p b j c", b=2), accv, ACT.Copy).then_inc(s_acc, 1)

            def step(i, s, first):
                n = i * HALF + s
                scale = float(1.0 / np.sqrt(DA if UNITS[s // STEPS][1] == "a" else DB))
                act.wait_ge(s_st, n + 1)
                if not (first and s < N32):
                    act.wait_ge(s_lo, n + 1 - N32)
                act.activation(p32[:, s % N32, :], st[:, s % 2, :, :].rearrange("p a b -> p (a b)"), ACT.Exp,
                               scale=scale).then_inc(s_exp, 1)
                act.wait_ge(s_exp, n + 1)
                if not (first and s < NP):
                    act.wait_ge(s_pv, n + 1 - NP)
                act.activation(ph[:, s % NP, :, :].rearrange("p a b -> p (a b)"), p32[:, s % N32, :], ACT.Copy).then_inc(s_hi, 1)

            def body(i, first, last):
                for s in range(HALF):
                    step(i, s, first)
                    if s % STEPS == 1 and not (first and s < STEPS):
                        before(i, s, copy_acc, first)

            loop(act, body)
            copy_acc(N - 1, 2, False)

        @block.vector
        def _(dve):
            def reduce(m, c, upar):
                dve.wait_ge(s_mx, m + 1)
                dve.tensor_reduce(part[:, upar, c:c + 1], mx[:, :, :].rearrange("p a b -> p (a b)"), AX, ALU.max).then_inc(s_red, 1)

            def max_done(u, upar):
                dve.wait_ge(s_red, u * 8 + 8)
                dve.tensor_reduce(rowmax[:, upar, :], part[:, upar, :].rearrange("p (j k) -> p j k", k=2), AX, ALU.max).then_inc(s_md, 1)
                dve.wait_ge(s_md, u * 3 + 1)
                dve.tensor_scalar(mpair[:, upar, :, 0], rowmax[:, upar, :], -1.0 / ONE, None, ALU.mult).then_inc(s_md, 1)
                dve.wait_ge(s_md, u * 3 + 2)
                dve.scalar_tensor_tensor(out=mpair[:, upar, :, 1], in0=rowmax[:, upar, :], scalar=-1.0 / ONE,
                                         in1=mpair[:, upar, :, 0], op0=ALU.mult, op1=ALU.subtract).then_inc(s_md, 1)

            def rows(u, pos):
                g, kind = UNITS[pos]
                dve.wait_ge(s_mt, u + 1)
                if kind == "a":
                    dve.tensor_copy(qa_lm[g][64:66, :], mx[64:66, 0, :]).then_inc(s_mr, 1)
                else:
                    dve.tensor_copy(qb_lm[DB:DB + 2, :], mx[DB:DB + 2, 0, :]).then_inc(s_mr, 1)

            def lo(i, s, first):
                n = i * HALF + s
                dve.wait_ge(s_hi, n + 1)
                if not (first and s < NP):
                    dve.wait_ge(s_pv, n + 1 - NP)
                dve.tensor_tensor(pl[:, s % NP, :, :].rearrange("p a b -> p (a b)"), p32[:, s % N32, :],
                                  ph[:, s % NP, :, :].rearrange("p a b -> p (a b)"), ALU.subtract).then_inc(s_lo, 1)

            def ahead(i, s, last):
                m = s + LEAD
                pos, c = m // STEPS, m % STEPS
                if last and pos > 2:
                    return
                u = i * 3 + pos
                reduce(u * 8 + c, c, pos % 3 % 2)
                if c == 7:
                    max_done(u, pos % 3 % 2)
                
            def row_step(i, s, last):
                m = s + LEAD - 8
                if m % STEPS == 1:
                    pos = m // STEPS
                    if not (last and pos > 2):
                        rows(i * 3 + pos, pos % 3)

            def denominator(i, pos, first):
                dve.wait_ge(s_acc, i * 3 + pos + 1)
                if not first:
                    dve.wait_ge(s_y, y_before(i, pos))
                dve.reciprocal(rden[:, :], acc_sb[:, :, 2 * DA]).then_inc(s_rden, 1)

            def body(i, first, last):
                for s in range(HALF):
                    ahead(i, s, last)
                    row_step(i, s, last)
                    lo(i, s, first)
                    if s % STEPS == 3 and not (first and s < STEPS):
                        before(i, s, denominator, first)

            for g in range(GA):
                dve.memset(ka_h1[g][64:66, :], ONE).then_inc(s_const, 1)
            dve.memset(kb_h1[DB:DB + 2, :], ONE).then_inc(s_const, 1)
            for m in range(LEAD):
                u, c = m // STEPS, m % STEPS
                reduce(m, c, u % 2)
                if c == 7:
                    max_done(u, u % 2)
                if c == 1 and u == 1:
                    rows(0, 0)
            loop(dve, body)
            denominator(N - 1, 2, False)

        @block.tensor
        def _(pe):
            def max_scores(u, pos, c, m, start):
                g, kind = UNITS[pos]
                if not start:
                    pe.wait_ge(s_red, m)
                j, half = c // 2, c % 2
                for b in range(2):
                    keys = slice(half * KW + b * QB, half * KW + (b + 1) * QB)
                    if kind == "a":
                        last = pe.matmul(mx[:, b, :], qa_hh[g][:, j * P:(j + 1) * P], ka_hl[g][:, keys], start=True, stop=True)
                    else:
                        last = pe.matmul(mx[:, b, :], qb_h[:, j * P:(j + 1) * P], kb_h1[0:DB, keys], start=True, stop=True)
                last.then_inc(s_mx, 1)

            def loaded(i, pos):
                g, kind = UNITS[pos]
                n = 48 if kind == "a" else 32
                pe.wait_ge(s_q[pos], i * n + n)
                if kind == "b":
                    pe.wait_ge(s_kb, i * 32 + 32)

            def turn(u, pos):
                kind = UNITS[pos][1]
                p0 = 64 if kind == "a" else DB
                pe.wait_ge(s_md, u * 3 + 3)
                for j in range(QT):
                    last = pe.matmul(mx[p0:p0 + 2, 0, j * P:(j + 1) * P], mpair[:, pos % 2, j, :], eye[:, :],
                                     start=True, stop=True)
                last.then_inc(s_mt, 1)

            def ahead(i, s, last):
                m = s + LEAD
                posn, c = m // STEPS, m % STEPS
                if last and posn > 2:
                    return
                pos, ii = posn % 3, (i + 1 if posn > 2 else i)
                u = i * 3 + posn
                if c == 0:
                    loaded(ii, pos)
                if c == 2:
                    pe.wait_ge(s_mr, u)
                max_scores(u, pos, c, u * 8 + c, False)

            def turn_step(i, s, last):
                m = s + LEAD - 8
                if m % STEPS == 1:
                    posn = m // STEPS
                    if not (last and posn > 2):
                        pe.wait_ge(s_red, i * HALF + s + LEAD + 1 if not (last and s + LEAD >= HALF) else N * HALF)
                        turn(i * 3 + posn, posn % 3)

            def scores(i, s, first):
                pos = s // STEPS
                g, kind = UNITS[pos]
                n = i * HALF + s
                if s % STEPS == 0:
                    pe.wait_ge(s_mr, i * 3 + pos + 1)
                if not (first and s < 2):
                    pe.wait_ge(s_exp, n - 1)
                for b in range(2):
                    k0 = (s % STEPS * 2 + b) * P
                    keys = slice(k0, k0 + P)
                    out = st[:, s % 2, b, :]
                    if kind == "a":
                        pe.matmul(out, ka_hl[g][:, keys], qa_hh[g][:, :], start=True, stop=False)
                        last = pe.matmul(out, ka_h1[g][:, keys], qa_lm[g][:, :], start=False, stop=True)
                    else:
                        pe.matmul(out, kb_h1[0:DB, keys], qb_h[:, :], start=True, stop=False)
                        pe.matmul(out, kb_l[:, keys], qb_h[:, :], start=False, stop=False)
                        last = pe.matmul(out, kb_h1[:, keys], qb_lm[:, :], start=False, stop=True)
                last.then_inc(s_st, 1)

            def pv(i, s, first):
                pos = s // STEPS
                g, kind = UNITS[pos % 3]
                n = i * HALF + s
                slot = s % NP
                k = s % STEPS
                if k == 0 and not (first and s == 0):
                    pe.wait_ge(s_acc, i * 3 + pos)
                if k == 0 and pos == 2:
                    pe.wait_ge(s_vb, i * 16 + 16)
                pe.wait_ge(s_hi, n + 1)
                pe.wait_ge(s_lo, n + 1)
                for b in range(2):
                    t = 2 * k + b
                    for j in range(QT):
                        hi, lo = ph[:, slot, b, j * P:(j + 1) * P], pl[:, slot, b, j * P:(j + 1) * P]
                        a = accv[:, j // 2, j % 2, :]
                        new, end = t == 0 and j % 2 == 0, t == TILES - 1
                        if kind == "a":
                            pe.matmul(a, hi, vas[:, t, g, :], start=new, stop=False, skip_group_check=True)
                            last = pe.matmul(a[:, DA:], lo, vas[:, t, g, DA:], start=False, stop=end, skip_group_check=True)
                        else:
                            pe.matmul(a, hi, vbs[:, t, DVB:], start=new, stop=False, skip_group_check=True)
                            pe.matmul(a[:, 0:DVB], hi, vbs[:, t, 0:DVB], start=False, stop=False, skip_group_check=True)
                            last = pe.matmul(a, lo, vbs[:, t, DVB:], start=False, stop=end, skip_group_check=True)
                last.then_inc(s_pv, 1)

            PVLAG = 2

            def body(i, first, last):
                for s in range(HALF):
                    ahead(i, s, last)
                    turn_step(i, s, last)
                    scores(i, s, first)
                    if not (first and s < PVLAG):
                        pv(i, s - PVLAG, first)

            pe.wait_ge(s_eye, 2)
            pe.wait_ge(s_const, 3)
            pe.wait_ge(s_ka, 96)
            for m in range(LEAD):
                u, c = m // STEPS, m % STEPS
                if c == 0:
                    loaded(0, u)
                if c == 2 and u == 1:
                    pe.wait_ge(s_mr, 1)
                max_scores(u, u, c, m, m == 0)
                if c == 1 and u == 1:
                    pe.wait_ge(s_red, m + 1)
                    turn(0, 0)
            pe.wait_ge(s_va, 16)
            loop(pe, body)
            pv(N - 1, HALF - 2, False)
            pv(N - 1, HALF - 1, False)


def phase3(nc, x, w_out, YA, YB, G, out):
    WS = 64.0
    with ExitStack() as ctx:
        sb = lambda n, s, d=F32: ctx.enter_context(nc.sbuf_tensor("p3_" + n, s, d))
        ps = lambda n, s, d=F32: ctx.enter_context(nc.psum_tensor("p3_" + n, s, d))
        sem = lambda n: ctx.enter_context(nc.semaphore("p3_" + n))

        w_raw = sb("w_raw", [P, KT, D])
        w_hi = sb("w_hi", [P, KT, D], F16)
        w_lo = sb("w_lo", [P, KT, D], F16)
        ya = sb("ya", [P, 2, HA, DA])
        yb = sb("yb", [P, 2, HB, DVB])
        gt = sb("gt", [P, 2, D])
        sg = sb("sg", [P, 2, D])
        xr = sb("xr", [P, 2, D])
        yg = sb("yg", [P, 2, D])
        yh = sb("yh", [P, D], F16)
        yl = sb("yl", [P, D], F16)
        yT = sb("yT", [P, 2, 2, KT, P], F16)
        res = sb("res", [P, 2, D])
        eye = sb("eye", [P, P], F16)
        tp = [ps(f"tp{s}", [P, KT, P], F16) for s in range(2)]
        po = [[ps(f"po{b}{c}", [P, 512]) for c in range(2)] for b in range(2)]

        s_w = [sem("w_loaded0"), sem("w_loaded1")]
        s_whi = sem("w_hi")
        s_wlo = sem("w_lo")
        s_eye = sem("eye_ready")
        s_y = [sem("y_loaded0"), sem("y_loaded1")]
        s_g = [sem("g_loaded0"), sem("g_loaded1")]
        s_x = [sem("x_loaded0"), sem("x_loaded1")]
        s_sg = sem("silu_done")
        s_yg = sem("y_gated")
        s_yh = sem("y_hi")
        s_yl = sem("y_lo")
        s_tp = sem("yT_in_psum")
        s_yt = sem("yT_in_sbuf")
        s_po = sem("out_in_psum")
        s_res = sem("residual_added")
        s_out = [sem("out_stored0"), sem("out_stored1")]

        xt = x.rearrange("b (t p) d -> (b t) p d", p=P)
        ot = out.rearrange("b (t p) d -> (b t) p d", p=P)
        wo = w_out.rearrange("l (k p) n -> (l p) k n", p=P)

        def loop(eng, body):
            for h in range(2):
                body(h, h, 0, True, False)
            with eng.Fori(1, PAIRS - 1) as i:
                for h in range(2):
                    body(i * 2 + h, h, i, False, False)
            for h in range(2):
                body(TILES - 2 + h, h, PAIRS - 1, False, True)

        block = ctx.enter_context(nc.Block())

        @block.sync
        def _(sp):
            def load_yg(t, h):
                for g in range(GA):
                    sp.dma_start(ya[:, h, g * 4:g * 4 + 4, :], YA[g].rearrange("h t p d -> t p h d")[t]).then_inc(s_y[h], 16)
                sp.dma_start(yb[:, h], YB.rearrange("h t p d -> t p h d")[t]).then_inc(s_y[h], 16)
                sp.dma_start(gt[:, h, :], G[t]).then_inc(s_g[h], 16)

            for t in range(2):
                load_yg(t, t)
                sp.dma_start(w_raw[:, :, t * 512:(t + 1) * 512], wo[:, :, t * 512:(t + 1) * 512]).then_inc(s_w[t], 16)
            for t in range(2):
                sp.dma_start(xr[:, t, :], xt[t]).then_inc(s_x[t], 16)

            def tile(t, h, i, first, last):
                if not last:
                    sp.wait_ge(s_yg, t * 2 + 2)
                    load_yg(t + 2, h)
                sp.wait_ge(s_res, t * 2 + 2)
                sp.dma_start(ot[t], res[:, h, :]).then_inc(s_out[h], 16)
                if not last:
                    sp.dma_start(xr[:, h, :], xt[t + 2]).then_inc(s_x[h], 16)

            loop(sp, tile)
            for h in range(2):
                sp.wait_ge(s_out[h], PAIRS * 16)

        @block.gpsimd
        def _(pool):
            pool.memset(eye[:, :], 0.0).then_inc(s_eye, 1)
            pool.wait_ge(s_eye, 1)
            pool.affine_select(out=eye[:, :], in_=eye[:, :], compare_op=ALU.not_equal, fill=1.0,
                               base=0, pattern=[[-1, P]], channel_multiplier=1).then_inc(s_eye, 1)

        @block.scalar
        def _(act):
            def silu(t, h, i, early):
                act.wait_ge(s_g[h], i * 16 + 16)
                if not early:
                    act.wait_ge(s_yg, t * 2 - 2)
                act.activation(sg[:, h, :], gt[:, h, :], ACT.Silu).then_inc(s_sg, 1)

            silu(0, 0, 0, True)
            for c in range(2):
                act.wait_ge(s_w[c], 16)
                cols = slice(c * 512, (c + 1) * 512)
                act.activation(w_hi[:, :, cols], w_raw[:, :, cols], ACT.Copy, scale=WS).then_inc(s_whi, 1)

            def tile(t, h, i, first, last):
                act.wait_ge(s_yg, t * 2 + 2)
                if not (first and h == 0):
                    act.wait_ge(s_tp, t * 2)
                act.activation(yh[:, :], yg[:, h, :], ACT.Copy).then_inc(s_yh, 1)
                if not (last and h == 1):
                    silu(t + 1, 1 - h, i if h == 0 else i + 1, first and h == 0)
                for s in range(2):
                    act.wait_ge(s_tp, t * 2 + s + 1)
                    if not first:
                        act.wait_ge(s_po, t * 2 - 2)
                    act.activation(yT[:, h, s], tp[s][:, :, :], ACT.Copy).then_inc(s_yt, 1)

            loop(act, tile)

        @block.vector
        def _(dve):
            def gate(t, h, i, early):
                dve.wait_ge(s_y[h], i * 48 + 48)
                dve.wait_ge(s_sg, t + 1)
                if not early:
                    dve.wait_ge(s_yh, t - 1)
                    dve.wait_ge(s_yl, t - 1)
                dve.tensor_tensor(yg[:, h, 0:512], ya[:, h].rearrange("p h d -> p (h d)"), sg[:, h, 0:512], ALU.mult).then_inc(s_yg, 1)
                dve.tensor_tensor(yg[:, h, 512:], yb[:, h].rearrange("p h d -> p (h d)"), sg[:, h, 512:], ALU.mult).then_inc(s_yg, 1)

            def residual(t, h, i, early):
                for c in range(2):
                    cols = slice(c * 512, (c + 1) * 512)
                    dve.wait_ge(s_po, t * 2 + c + 1)
                    dve.wait_ge(s_x[h], i * 16 + 16)
                    if not early:
                        dve.wait_ge(s_out[h], i * 16)
                    dve.scalar_tensor_tensor(out=res[:, h, cols], in0=po[h][c][:, :], scalar=1.0 / WS, in1=xr[:, h, cols],
                                             op0=ALU.mult, op1=ALU.add).then_inc(s_res, 1)

            gate(0, 0, 0, True)
            for c in range(2):
                cols = slice(c * 512, (c + 1) * 512)
                dve.wait_ge(s_whi, c + 1)
                dve.scalar_tensor_tensor(out=w_lo[:, :, cols], in0=w_raw[:, :, cols], scalar=WS,
                                         in1=w_hi[:, :, cols], op0=ALU.mult, op1=ALU.subtract).then_inc(s_wlo, 1)

            def tile(t, h, i, first, last):
                dve.wait_ge(s_yh, t + 1)
                if not (first and h == 0):
                    dve.wait_ge(s_tp, t * 2)
                dve.tensor_tensor(yl[:, :], yg[:, h, :], yh[:, :], ALU.subtract).then_inc(s_yl, 1)
                if not (last and h == 1):
                    gate(t + 1, 1 - h, i if h == 0 else i + 1, first and h == 0)
                if not (first and h == 0):
                    residual(t - 1, 1 - h, i - 1 if h == 0 else i, first or (isinstance(i, int) and i == 0))

            loop(dve, tile)
            residual(TILES - 1, 1, PAIRS - 1, False)

        @block.tensor
        def _(pe):
            def turn(t, first):
                for s, src in enumerate((yh, yl)):
                    pe.wait_ge(s_yh if s == 0 else s_yl, t + 1)
                    if not first:
                        pe.wait_ge(s_yt, t * 2 - 1 + s)
                    for k in range(KT):
                        last = pe.transpose(tp[s][:, k, :], src[:, k * P:(k + 1) * P], eye[:, :])
                    last.then_inc(s_tp, 1)

            def tile(t, h, i, first, last):
                pe.wait_ge(s_yt, t * 2 + 2)
                for c in range(2):
                    cols = slice(c * 512, (c + 1) * 512)
                    if first and h == 0:
                        pe.wait_ge(s_wlo, c + 1)
                    if not first:
                        pe.wait_ge(s_res, t * 2 - 3 + c)
                    for k in range(KT):
                        for m, (s, w) in enumerate(((0, w_hi), (0, w_lo), (1, w_hi))):
                            mm = pe.matmul(po[h][c][:, :], yT[:, h, s, k, :], w[:, k, cols],
                                           start=(k == 0 and m == 0), stop=(k == KT - 1 and m == 2))
                    mm.then_inc(s_po, 1)
                    if c == 0 and not (last and h == 1):
                        turn(t + 1, False)

            pe.wait_ge(s_eye, 2)
            turn(0, True)
            loop(pe, tile)


def layer(nc, x, w_in, w_uq, w_ukv, g_in, g_cq, g_ckv, g_heads, trig, eye, w_out, out):
    dram = lambda n, s, d=F16: nc.dram_tensor("scratch_" + n, s, d, kind="Internal").ap()
    QA = dram("qa", [2, HA, PAIRS, DA, 2 * P])
    KA = dram("ka", [2, GA, PAIRS, DA, 2 * P])
    QBd = dram("qb", [2, HB, PAIRS, DB, 2 * P])
    KBd = dram("kb", [2, HB, PAIRS, DB, 2 * P])
    VA = dram("va", [TILES, P, GA, 2 * DA + 1])
    VB = dram("vb", [TILES, P, HB, 2 * DVB + 1])
    G = dram("g", [TILES, P, D], F32)
    YA = dram("ya", [GA, HB, TILES, P, DA], F32)
    YB = dram("yb", [HB, TILES, P, DVB], F32)
    phase1(nc, x, w_in, w_uq, w_ukv, g_in, g_cq, g_ckv, g_heads, trig, eye, QA, KA, QBd, KBd, VA, VB, G)
    phase2(nc, QA, KA, QBd, KBd, VA, VB, YA, YB)
    phase3(nc, x, w_out, YA, YB, G, out)


def kernel(**inputs):
    import concourse.bacc as _bacc
    from concourse.bass_utils import run_bass_kernel_spmd as _run

    a = {k: np.ascontiguousarray(v) for k, v in inputs.items()}
    heads = [a["a_q_norm"]] * HA + [a["a_k_norm"]] * GA + [a["b_q_norm"]] * HB + [a["b_k_norm"]] * HB
    named = {
        "x": a["x"], "w_in": a["w_in"], "w_uq": a["w_uq"], "w_ukv": a["w_ukv"], "g_in": a["norm_in"],
        "g_cq": a["b_cq_norm"], "g_ckv": a["b_ckv_norm"], "g_heads": np.concatenate(heads, axis=1).reshape(NZ),
        "trig": rope_tables(), "eye": np.eye(P, dtype=np.float32), "w_out": a["w_out"],
    }
    nc = _bacc.Bacc("TRN2", target_bir_lowering=False, num_devices=1)
    arrays, args = {}, []
    for name, v in named.items():
        arrays[f"in_{name}"] = v
        args.append(nc.dram_tensor(f"in_{name}", v.shape, mybir.dt.from_np(v.dtype), kind="ExternalInput").ap())
    args.append(nc.dram_tensor("out_0", (1, SEQ, D), F32, kind="ExternalOutput").ap())
    layer(nc, *args)
    r = _run(nc, [arrays], core_ids=[0])
    return r.results[0]["out_0"]
```

```python
from contextlib import ExitStack

import numpy as np
import concourse.bass as bass
from concourse import mybir

F32 = mybir.dt.float32
F16 = mybir.dt.float16
ALU = mybir.AluOpType
ACT = mybir.ActivationFunctionType
AX = mybir.AxisListType.X

P = 128
SEQ, D = 2048, 1024
EPS = 1e-6
GRID_W, THETA = 64, 10000.0
HA, GA, DA = 8, 2, 64
HB, NOPE, ROPE, DVB = 4, 64, 32, 128
DB = NOPE + ROPE
RQ, RKV = 384, 256
NIN = 2464
KT = D // P
TILES = SEQ // P
PAIRS = TILES // 2
QB = 512
NQ = SEQ // QB
QT = QB // P

CAK, CBQ, CBK, NZ = 512, 640, 1024, 1408
CHUNKS = [128 * c for c in range(5)] + [CBQ + DB * c for c in range(8)]
NZP = CHUNKS[-1] + P
NCH = len(CHUNKS)
PROJ = {"cq": (1280, 384), "ckv": (1664, 288), "aq": (0, 512), "akv": (512, 256), "ag": (768, 512), "bg": (1952, 512)}
PORDER = ["cq", "ckv", "aq", "akv", "ag", "bg"]


def rope_tables():
    rows = SEQ // GRID_W
    row = np.repeat(np.arange(rows, dtype=np.float32), GRID_W)
    col = np.tile(np.arange(GRID_W, dtype=np.float32), rows)
    out = []
    for dim in (DA, ROPE):
        half = dim // 2
        inv = (1.0 / (np.float32(THETA) ** (np.arange(0, half, 2, dtype=np.float32) / np.float32(half)))).astype(np.float32)
        ar, ac = row[:, None] * inv[None, :], col[:, None] * inv[None, :]
        out.append(np.concatenate([np.cos(ar), np.cos(ar), np.cos(ac), np.cos(ac)], 1))
        out.append(np.concatenate([-np.sin(ar), np.sin(ar), -np.sin(ac), np.sin(ac)], 1))
    return np.concatenate(out, 1).astype(np.float32)


def phase1(nc, x, w_in, w_uq, w_ukv, g_in, g_cq, g_ckv, g_heads, trig, eye, QA, KA, QBd, KBd, VA, VB, G):
    with ExitStack() as ctx:
        sb = lambda n, s, d=F32: ctx.enter_context(nc.sbuf_tensor("p1_" + n, s, d))
        ps = lambda n, s, d=F32: ctx.enter_context(nc.psum_tensor("p1_" + n, s, d))
        sem = lambda n: ctx.enter_context(nc.semaphore("p1_" + n))

        w_hi = sb("w_hi", [P, KT, NIN], F16)
        w_lo = sb("w_lo", [P, KT, NIN], F16)
        w_raw = sb("w_raw", [P, 2, KT * 512])
        uq_hi = sb("uq_hi", [P, 3, HB * DB], F16)
        uq_lo = sb("uq_lo", [P, 3, HB * DB], F16)
        ukv_hi = sb("ukv_hi", [P, 2, HB * (NOPE + DVB)], F16)
        ukv_lo = sb("ukv_lo", [P, 2, HB * (NOPE + DVB)], F16)
        gin = sb("gin", [P, KT])
        gcq = sb("gcq", [P, 3])
        gckv = sb("gckv", [P, 2])
        gains = sb("gains", [P, NZ])
        eye32 = sb("eye32", [P, P])
        ident = sb("ident", [P, P], F16)
        eps = sb("eps", [P, 1])
        xin = sb("xin", [P, 2, D])
        trg = sb("trg", [P, 2, 192])
        stat = sb("stat", [P, 2, 8])
        lstat = sb("lstat", [P, 2, 8])
        xh = sb("xh", [P, D], F16)
        xl = sb("xl", [P, D], F16)
        junk = sb("junk", [P, D])
        xT = sb("xT", [P, 2, 2, KT, P], F16)
        cq32 = sb("cq32", [P, RQ])
        ckv32 = sb("ckv32", [P, RKV + ROPE])
        lat_hi = sb("lat_hi", [P, RQ + RKV], F16)
        lat_lo = sb("lat_lo", [P, RQ + RKV], F16)
        latT = sb("latT", [P, 10, P], F16)
        R = sb("R", [P, 2, NZ])
        sq = sb("sq", [P, NZ])
        rstat = sb("rstat", [P, 6, 18])
        T2 = sb("T2", [P, CBQ + 8 * ROPE])
        zh = sb("zh", [P, NZP], F16)
        zl = sb("zl", [P, NZP], F16)
        zT = sb("zT", [P, 2 * NCH, 2 * P], F16)
        va32 = sb("va32", [P, GA * DA])
        vb32 = sb("vb32", [P, HB, DVB])
        va = sb("va", [P, GA, 2 * DA + 1], F16)
        vb = sb("vb", [P, HB, 2 * DVB + 1], F16)
        g32 = sb("g32", [P, D])

        ring = [ps(f"ring{i}", [P, 512]) for i in range(3)]
        xtp = [ps(f"xtp{i}", [P, KT, P], F16) for i in range(2)]
        trp = [ps(f"trp{i}", [P, KT, P], F16) for i in range(3)]

        s_const = sem("const_loaded")
        s_gains = sem("gains_loaded")
        s_x = [sem("x_loaded0"), sem("x_loaded1")]
        s_trig = [sem("trig_loaded0"), sem("trig_loaded1")]
        s_w = [sem("w_loaded0"), sem("w_loaded1")]
        s_whi = sem("w_hi_split")
        s_wlo = sem("w_lo_split")
        s_ident = sem("ident_ready")
        s_eps = sem("eps_ready")
        s_ones = sem("ones_ready")
        s_ax = sem("act_x_chain")
        s_dx = sem("dve_x")
        s_xtp = sem("xT_in_psum")
        s_xt = sem("xT_in_sbuf")
        s_proj = sem("proj_done")
        s_ring = sem("ring_read")
        s_lat = sem("act_latents")
        s_dlat = sem("dve_latents")
        s_ltp = sem("latT_in_psum")
        s_lt = sem("latT_in_sbuf")
        s_R = sem("R_written")
        s_sq = sem("R_squared")
        s_hsum = sem("head_sums")
        s_hdev = sem("head_deviations")
        s_rc = sem("rope_chain")
        s_zh = sem("z_hi")
        s_zl = sem("z_lo")
        s_zp = sem("zT_in_psum")
        s_zt = sem("zT_in_sbuf")
        s_zst = sem("zT_stored")
        s_v32 = sem("v_raw")
        s_vhi = sem("v_hi")
        s_vlo = sem("v_lo")
        s_vst = sem("v_stored")
        s_gst = sem("gate_stored")
        RC = 9
        ZST = 12 * 16
        ZG = [(0, 7), (7, 13), (13, 20), (20, 26)]

        xt = x.rearrange("b (t p) d -> (b t) p d", p=P)
        trt = trig.rearrange("(t p) c -> t p c", p=P)
        w3 = w_in.rearrange("l (k p) n -> (l p) k n", p=P)

        pieces = []
        for name in PORDER[0:5] + ["uq", "ukv"] + PORDER[5:]:
            raw = w_raw[:, len(pieces) % 2, :]
            if name in PROJ:
                c0, w = PROJ[name]
                pieces.append((raw[:, 0:KT * w].rearrange("p (k n) -> p k n", k=KT), w3[:, :, c0:c0 + w], gin,
                               w_hi[:, :, c0:c0 + w], w_lo[:, :, c0:c0 + w]))
            elif name == "uq":
                pieces.append((raw[:, 0:3 * 384].rearrange("p (k n) -> p k n", k=3),
                               w_uq.rearrange("l (k p) n -> (l p) k n", p=P), gcq, uq_hi, uq_lo))
            else:
                pieces.append((raw[:, 0:2 * 768].rearrange("p (k n) -> p k n", k=2),
                               w_ukv.rearrange("l (k p) n -> (l p) k n", p=P), gckv, ukv_hi, ukv_lo))
        PIECE = {"cq": 1, "ckv": 2, "aq": 3, "akv": 4, "ag": 5, "uq": 6, "ukv": 7, "bg": 8}

        def loop(eng, body):
            body(0, True, False)
            with eng.Fori(1, PAIRS - 1) as i:
                body(i, False, False)
            body(PAIRS - 1, False, True)

        block = ctx.enter_context(nc.Block())

        @block.sync
        def _(sp):
            sp.dma_start(xin[:, 0, :], xt[0]).then_inc(s_x[0], 16)
            sp.dma_start(gin[:, :], g_in.rearrange("l (k p) -> (l p) k", p=P), allow_slow_non_contiguous=True).then_inc(s_const, 16)
            sp.dma_start(eye32[:, :], eye).then_inc(s_const, 16)
            sp.dma_start(gcq[:, :], g_cq.rearrange("l (k p) -> (l p) k", p=P), allow_slow_non_contiguous=True).then_inc(s_const, 16)
            sp.dma_start(gckv[:, :], g_ckv.rearrange("l (k p) -> (l p) k", p=P), allow_slow_non_contiguous=True).then_inc(s_const, 16)
            for n, (raw, src, gain, hi, lo) in enumerate(pieces):
                if n >= 2:
                    sp.wait_ge(s_whi, n - 1)
                    sp.wait_ge(s_wlo, n - 1)
                sp.dma_start(raw, src).then_inc(s_w[n % 2], 16)
                if n == 1:
                    sp.dma_start(xin[:, 1, :], xt[1]).then_inc(s_x[1], 16)
                    sp.dma_start(trg[:, 0, :], trt[0]).then_inc(s_trig[0], 16)
                    sp.dma_start(gains[:, :], g_heads.partition_broadcast(P)).then_inc(s_gains, 16)

            def tile(i, h, first, last):
                t = i * 2 + h
                if not (last and h == 1):
                    if not (first and h == 0):
                        sp.wait_ge(s_rc, t * RC)
                    sp.dma_start(trg[:, 1 - h, :], trt[t + 1]).then_inc(s_trig[1 - h], 16)
                if not last:
                    sp.wait_ge(s_dx, t * 2 + 2)
                    sp.dma_start(xin[:, h, :], xt[t + 2]).then_inc(s_x[h], 16)
                if h == 0 and not first:
                    sp.wait_ge(s_zt, t * 4)
                    store_z(i - 1)
                sp.wait_ge(s_vhi, t + 1)
                sp.wait_ge(s_vlo, t + 1)
                sp.dma_start(VA[t], va[:, :, :]).then_inc(s_vst, 16)
                sp.dma_start(VB[t], vb[:, :, :]).then_inc(s_vst, 16)
                sp.wait_ge(s_ring, t * 9 + 9)
                sp.dma_start(G[t], g32[:, :]).then_inc(s_gst, 16)

            def store_z(pr):
                for s in range(2):
                    for h2 in range(2):
                        rows = slice(64 * h2, 64 * h2 + 64)
                        sp.dma_start(QA[s].rearrange("(c h) pr r t -> h pr r c t", h=2)[h2, pr],
                                     zT[rows, NCH * s:NCH * s + 4, :]).then_inc(s_zst, 16)
                        sp.dma_start(KA[s, h2, pr], zT[rows, NCH * s + 4, :]).then_inc(s_zst, 16)
                    sp.dma_start(QBd[s].rearrange("h pr r t -> pr r h t")[pr],
                                 zT[0:DB, NCH * s + 5:NCH * s + 9, :]).then_inc(s_zst, 16)
                    sp.dma_start(KBd[s].rearrange("h pr r t -> pr r h t")[pr],
                                 zT[0:DB, NCH * s + 9:NCH * s + 13, :]).then_inc(s_zst, 16)

            loop(sp, lambda i, first, last: [tile(i, h, first, last) for h in range(2)])
            sp.wait_ge(s_zt, TILES * 4)
            store_z(PAIRS - 1)
            sp.wait_ge(s_zst, PAIRS * ZST)
            sp.wait_ge(s_vst, TILES * 32)
            sp.wait_ge(s_gst, TILES * 16)

        @block.gpsimd
        def _(pool):
            pool.memset(va[:, :, 2 * DA:2 * DA + 1], 1.0).then_inc(s_ones, 1)
            pool.memset(vb[:, :, 2 * DVB:2 * DVB + 1], 1.0).then_inc(s_ones, 1)
            pool.memset(zh[:, NZ:], 0.0).then_inc(s_ones, 1)
            pool.memset(zl[:, NZ:], 0.0).then_inc(s_ones, 1)

        @block.scalar
        def _(act):
            def x_hi(t, h):
                st = stat[:, h, :]
                act.wait_ge(s_x[h], x_count(t, h))
                act.activation(junk[:, 0:D], xin[:, h, :], ACT.Square, accum_out=st[:, 0:1]).then_inc(s_ax, 1)
                act.wait_ge(s_ax, t * 3 + 1)
                act.activation(st[:, 1:2], st[:, 0:1], ACT.Sqrt, bias=eps[:, :], scale=1.0 / D).then_inc(s_ax, 1)
                act.wait_ge(s_dx, t * 2 + 1)
                if not zero(t):
                    act.wait_ge(s_xtp, t * 2)
                act.activation(xh[:, :], xin[:, h, :], ACT.Copy, scale=st[:, 2:3]).then_inc(s_ax, 1)

            def evac(t, n, *pairs):
                act.wait_ge(s_proj, t * 9 + n + 1)
                for dst, src in pairs:
                    last = act.activation(dst, src, ACT.Copy)
                last.then_inc(s_ring, 1)

            def z_hi(t, h):
                act.wait_ge(s_rc, t * RC + RC)
                if not zero(t):
                    act.wait_ge(s_zp, t * 4)
                act.activation(zh[:, 0:NZ], R[:, h, :], ACT.Copy).then_inc(s_zh, 1)

            def z_evac(t, h, pair):
                for n, (a, b) in enumerate(ZG):
                    act.wait_ge(s_zp, t * 4 + n + 1)
                    if n == 0 and h == 0 and pair is not None:
                        act.wait_ge(s_zst, pair * ZST)
                    act.activation(zT[:, a:b, P * h:P * h + P], trp[n % 3][:, 0:b - a, :], ACT.Copy).then_inc(s_zt, 1)

            def split_hi(n):
                raw, src, gain, hi, lo = pieces[n]
                act.wait_ge(s_w[n % 2], n // 2 * 16 + 16)
                for k in range(raw.shape[1]):
                    op = act.activation(hi[:, k, :], raw[:, k, :], ACT.Copy, scale=gain[:, k:k + 1])
                op.then_inc(s_whi, 1)

            def tile(i, h, first, last):
                t = i * 2 + h
                Rh = R[:, h, :]
                new = first and h == 0
                if not (last and h == 1):
                    x_hi(t + 1, 1 - h)
                if not (first and h == 0):
                    z_hi(t - 1, 1 - h)
                ls = lstat[:, h, :]
                if not (first and h == 0):
                    act.wait_ge(s_dlat, t * 2)
                evac(t, 0, (cq32[:, :], ring[0][:, 0:RQ]))
                evac(t, 1, (ckv32[:, :], ring[1][:, 0:RKV + ROPE]))
                act.wait_ge(s_ring, t * 9 + 2)
                act.activation(junk[:, 0:RQ], cq32[:, :], ACT.Square, accum_out=ls[:, 0:1]).then_inc(s_lat, 1)
                act.activation(junk[:, RQ:RQ + RKV], ckv32[:, 0:RKV], ACT.Square, accum_out=ls[:, 1:2]).then_inc(s_lat, 1)
                act.wait_ge(s_lat, t * 5 + 2)
                act.activation(ls[:, 2:3], ls[:, 0:1], ACT.Sqrt, bias=eps[:, :], scale=1.0 / RQ).then_inc(s_lat, 1)
                act.activation(ls[:, 3:4], ls[:, 1:2], ACT.Sqrt, bias=eps[:, :], scale=1.0 / RKV).then_inc(s_lat, 1)
                if new:
                    split_hi(3)
                act.wait_ge(s_dlat, t * 2 + 1)
                if not (first and h == 0):
                    act.wait_ge(s_ltp, t * 2)
                act.activation(lat_hi[:, 0:RQ], cq32[:, :], ACT.Copy, scale=ls[:, 4:5])
                act.activation(lat_hi[:, RQ:], ckv32[:, 0:RKV], ACT.Copy, scale=ls[:, 5:6]).then_inc(s_lat, 1)
                evac(t, 2, (Rh[:, 0:512], ring[2][:, :]))
                if new:
                    split_hi(4)
                if not (first and h == 0):
                    act.wait_ge(s_vlo, t)
                evac(t, 3, (Rh[:, CAK:CBQ], ring[0][:, 0:128]), (va32[:, :], ring[0][:, 128:256]))
                if new:
                    split_hi(5)
                    split_hi(6)
                if not (first and h == 0):
                    act.wait_ge(s_gst, t * 16)
                evac(t, 4, (g32[:, 0:512], ring[1][:, :]))
                kb = Rh[:, CBK:NZ].rearrange("p (h d) -> p h d", d=DB)
                act.activation(kb[:, :, NOPE:DB], ckv32[:, RKV:RKV + ROPE].unsqueeze(1).to_broadcast([P, HB, ROPE]), ACT.Copy)
                evac(t, 5, (Rh[:, CBQ:CBK], ring[2][:, 0:384]))
                for n in range(2):
                    r = ring[n][:, 0:384].rearrange("p (h d) -> p h d", d=NOPE + DVB)
                    evac(t, 6 + n, (vb32[:, 2 * n:2 * n + 2, :], r[:, :, NOPE:]), (kb[:, 2 * n:2 * n + 2, 0:NOPE], r[:, :, 0:NOPE]))
                if new:
                    split_hi(7)
                else:
                    z_evac(t - 1, 1 - h, i if h == 1 and not first else None)
                act.wait_ge(s_ring, t * 9 + 8)
                if not (first and h == 0):
                    act.wait_ge(s_hsum, t * 2)
                act.activation(sq[:, :], Rh, ACT.Square).then_inc(s_sq, 1)
                if first and h == 0:
                    act.wait_ge(s_ones, 2)
                else:
                    act.wait_ge(s_vst, t * 32)
                act.activation(va[:, :, DA:2 * DA], va32[:, :].rearrange("p (g d) -> p g d", d=DA), ACT.Copy)
                act.activation(vb[:, :, DVB:2 * DVB], vb32[:, :, :], ACT.Copy).then_inc(s_vhi, 1)
                act.wait_ge(s_hsum, t * 2 + 2)
                act.activation(rstat[:, 1, 0:10], rstat[:, 0, 0:10], ACT.Sqrt, bias=eps[:, :], scale=1.0 / DA)
                act.activation(rstat[:, 1, 10:18], rstat[:, 0, 10:18], ACT.Sqrt, bias=eps[:, :], scale=1.0 / DB).then_inc(s_hdev, 1)
                act.wait_ge(s_proj, t * 9 + 9)
                act.activation(g32[:, 512:], ring[2][:, :], ACT.Copy).then_inc(s_ring, 1)

            act.wait_ge(s_const, 64)
            act.activation(ident[:, :], eye32[:, :], ACT.Copy).then_inc(s_ident, 1)
            act.wait_ge(s_eps, 1)
            x_hi(0, 0)
            for n in range(3):
                split_hi(n)
            loop(act, lambda i, first, last: [tile(i, h, first, last) for h in range(2)])
            z_hi(TILES - 1, 1)
            z_evac(TILES - 1, 1, None)

        @block.vector
        def _(dve):
            def x_rstd(t, h):
                dve.wait_ge(s_ax, t * 3 + 2)
                dve.reciprocal(stat[:, h, 2:3], stat[:, h, 1:2]).then_inc(s_dx, 1)

            def x_lo(t, h):
                dve.wait_ge(s_dx, t * 2 + 1)
                dve.wait_ge(s_ax, t * 3 + 3)
                if not zero(t):
                    dve.wait_ge(s_xtp, t * 2)
                dve.scalar_tensor_tensor(out=xl[:, :], in0=xin[:, h, :], scalar=stat[:, h, 2:3], in1=xh[:, :],
                                         op0=ALU.mult, op1=ALU.subtract).then_inc(s_dx, 1)

            def xt_evac(t, h):
                for s in range(2):
                    dve.wait_ge(s_xtp, t * 2 + s + 1)
                    dve.tensor_copy(xT[:, h, s], xtp[s][:, :, :]).then_inc(s_xt, 1)

            def z_lo(t, h):
                dve.wait_ge(s_zh, t + 1)
                if not zero(t):
                    dve.wait_ge(s_zp, t * 4)
                dve.tensor_tensor(zl[:, 0:NZ], R[:, h, :], zh[:, 0:NZ], ALU.subtract).then_inc(s_zl, 1)

            def split_lo(n):
                raw, src, gain, hi, lo = pieces[n]
                dve.wait_ge(s_whi, n + 1)
                for k in range(raw.shape[1]):
                    op = dve.scalar_tensor_tensor(out=lo[:, k, :], in0=raw[:, k, :], scalar=gain[:, k:k + 1],
                                                  in1=hi[:, k, :], op0=ALU.mult, op1=ALU.subtract)
                op.then_inc(s_wlo, 1)

            def tile(i, h, first, last):
                t = i * 2 + h
                Rh = R[:, h, :]
                if not (last and h == 1):
                    x_rstd(t + 1, 1 - h)
                if not (first and h == 0):
                    z_lo(t - 1, 1 - h)
                if not (last and h == 1):
                    x_lo(t + 1, 1 - h)
                ls = lstat[:, h, :]
                dve.wait_ge(s_lat, t * 5 + 4)
                dve.reciprocal(ls[:, 4:6], ls[:, 2:4]).then_inc(s_dlat, 1)
                if first and h == 0:
                    split_lo(3)
                dve.wait_ge(s_dlat, t * 2 + 1)
                dve.wait_ge(s_lat, t * 5 + 5)
                dve.scalar_tensor_tensor(out=lat_lo[:, 0:RQ], in0=cq32[:, :], scalar=ls[:, 4:5], in1=lat_hi[:, 0:RQ],
                                         op0=ALU.mult, op1=ALU.subtract)
                dve.scalar_tensor_tensor(out=lat_lo[:, RQ:], in0=ckv32[:, 0:RKV], scalar=ls[:, 5:6], in1=lat_hi[:, RQ:],
                                         op0=ALU.mult, op1=ALU.subtract).then_inc(s_dlat, 1)
                dve.wait_ge(s_ltp, t * 2 + 1)
                dve.tensor_copy(latT[:, 0:6, :], trp[0][:, 0:6, :])
                dve.wait_ge(s_ltp, t * 2 + 2)
                dve.tensor_copy(latT[:, 6:10, :], trp[1][:, 0:4, :]).then_inc(s_lt, 1)
                if first and h == 0:
                    for n in range(4, 8):
                        split_lo(n)
                if not (last and h == 1):
                    xt_evac(t + 1, 1 - h)
                dve.wait_ge(s_sq, t + 1)
                if not (first and h == 0):
                    dve.wait_ge(s_hdev, t)
                dve.tensor_reduce(rstat[:, 0, 0:10], sq[:, 0:CBQ].rearrange("p (h d) -> p h d", d=DA), AX, ALU.add).then_inc(s_hsum, 1)
                dve.tensor_reduce(rstat[:, 0, 10:18], sq[:, CBQ:].rearrange("p (h d) -> p h d", d=DB), AX, ALU.add).then_inc(s_hsum, 1)
                dve.wait_ge(s_vhi, t + 1)
                dve.tensor_tensor(va[:, :, 0:DA], va32[:, :].rearrange("p (g d) -> p g d", d=DA), va[:, :, DA:2 * DA], ALU.subtract)
                dve.tensor_tensor(vb[:, :, 0:DVB], vb32[:, :, :], vb[:, :, DVB:2 * DVB], ALU.subtract).then_inc(s_vlo, 1)
                dve.wait_ge(s_hdev, t + 1)
                for a, b, n in ((0, 10, DA), (10, 18, DB)):
                    dve.tensor_scalar(rstat[:, 3, a:b], rstat[:, 0, a:b], 1.0 / n, EPS, ALU.mult, ALU.add)
                dve.reciprocal(rstat[:, 2, :], rstat[:, 1, :]).then_inc(s_rc, 1)
                dve.wait_ge(s_rc, t * RC + 1)
                dve.tensor_tensor(rstat[:, 4, :], rstat[:, 2, :], rstat[:, 3, :], ALU.mult).then_inc(s_rc, 1)
                dve.wait_ge(s_rc, t * RC + 2)
                dve.scalar_tensor_tensor(out=rstat[:, 5, :], in0=rstat[:, 4, :], scalar=-0.5, in1=rstat[:, 2, :],
                                         op0=ALU.mult, op1=ALU.mult).then_inc(s_rc, 1)
                dve.wait_ge(s_rc, t * RC + 3)
                dve.scalar_tensor_tensor(out=rstat[:, 2, :], in0=rstat[:, 5, :], scalar=1.5, in1=rstat[:, 2, :],
                                         op0=ALU.add, op1=ALU.mult).then_inc(s_rc, 1)
                dve.wait_ge(s_rc, t * RC + 4)
                ra = Rh[:, 0:CBQ].rearrange("p (h d) -> p h d", d=DA)
                rb = Rh[:, CBQ:].rearrange("p (h d) -> p h d", d=DB)
                dve.tensor_tensor(ra, ra, rstat[:, 2, 0:10].unsqueeze(2).to_broadcast([P, 10, DA]), ALU.mult)
                dve.tensor_tensor(rb, rb, rstat[:, 2, 10:18].unsqueeze(2).to_broadcast([P, 8, DB]), ALU.mult).then_inc(s_rc, 1)
                dve.wait_ge(s_rc, t * RC + 5)
                if first and h == 0:
                    dve.wait_ge(s_gains, 16)
                dve.tensor_tensor(Rh, Rh, gains[:, :], ALU.mult).then_inc(s_rc, 1)
                dve.wait_ge(s_rc, t * RC + 6)
                dve.wait_ge(s_trig[h], i * 16 + 16)
                tr = trg[:, h, :]
                parts = ((ra, T2[:, 0:CBQ].rearrange("p (h d) -> p h d", d=DA), 10, 0, 64),
                         (rb[:, :, NOPE:], T2[:, CBQ:].rearrange("p (h d) -> p h d", d=ROPE), 8, 128, 32))
                for r, t2, nh, c0, w in parts:
                    c = w // 4
                    rv = r.rearrange("p h (a f c) -> p h a f c", a=2, f=2)
                    tv = t2.rearrange("p h (a f c) -> p h a f c", a=2, f=2)
                    sv = tr[:, c0 + w:c0 + 2 * w].rearrange("p (a f c) -> p a f c", a=2, f=2)
                    for f in range(2):
                        last_op = dve.tensor_tensor(tv[:, :, :, f, :], rv[:, :, :, 1 - f, :],
                                                    sv[:, :, f, :].unsqueeze(1).to_broadcast([P, nh, 2, c]), ALU.mult)
                last_op.then_inc(s_rc, 1)
                dve.wait_ge(s_rc, t * RC + 7)
                for r, t2, nh, c0, w in parts:
                    last_op = dve.tensor_tensor(r, r, tr[:, c0:c0 + w].unsqueeze(1).to_broadcast([P, nh, w]), ALU.mult)
                last_op.then_inc(s_rc, 1)
                dve.wait_ge(s_rc, t * RC + 8)
                for r, t2, nh, c0, w in parts:
                    last_op = dve.tensor_tensor(r, r, t2, ALU.add)
                last_op.then_inc(s_rc, 1)

            dve.memset(eps[:, :], EPS).then_inc(s_eps, 1)
            x_rstd(0, 0)
            x_lo(0, 0)
            xt_evac(0, 0)

            dve.wait_ge(s_const, 64)
            for n in range(3):
                split_lo(n)
            loop(dve, lambda i, first, last: [tile(i, h, first, last) for h in range(2)])
            z_lo(TILES - 1, 1)

        @block.tensor
        def _(pe):
            def project(t, n, w, terms, new):
                if not (new and n < 3):
                    pe.wait_ge(s_ring, t * 9 + n - 2)
                for m, (a, b) in enumerate(terms):
                    last = pe.matmul(ring[n % 3][:, 0:w], a, b, start=(m == 0), stop=(m == len(terms) - 1))
                last.then_inc(s_proj, 1)

            def proj_in(t, h, name, n, new):
                c0, w = PROJ[name]
                if new:
                    pe.wait_ge(s_whi, PIECE[name])
                    pe.wait_ge(s_wlo, PIECE[name])
                cols = slice(c0, c0 + w)
                terms = []
                for k in range(KT):
                    terms += [(xT[:, h, 0, k, :], w_hi[:, k, cols]), (xT[:, h, 0, k, :], w_lo[:, k, cols]),
                              (xT[:, h, 1, k, :], w_hi[:, k, cols])]
                project(t, n, w, terms, new)

            def transpose_x(t, h):
                for s, src in enumerate((xh, xl)):
                    if s == 0:
                        pe.wait_ge(s_ax, t * 3 + 3)
                    else:
                        pe.wait_ge(s_dx, t * 2 + 2)
                    if not zero(t):
                        pe.wait_ge(s_xt, t * 2 - 1 + s)
                    for k in range(KT):
                        last = pe.transpose(xtp[s][:, k, :], src[:, k * P:(k + 1) * P], ident[:, :])
                    last.then_inc(s_xtp, 1)

            def transpose_latents(t, new):
                pe.wait_ge(s_lat, t * 5 + 5)
                pe.wait_ge(s_dlat, t * 2 + 2)
                if not new:
                    pe.wait_ge(s_lt, t)
                for b, (c0, nk) in enumerate(((0, 3), (RQ, 2))):
                    for s, src in enumerate((lat_hi, lat_lo)):
                        for k in range(nk):
                            last = pe.transpose(trp[b][:, s * nk + k, :], src[:, c0 + k * P:c0 + (k + 1) * P], ident[:, :])
                    last.then_inc(s_ltp, 1)

            def transpose_z(t, after, groups):
                if groups[0] == 0:
                    pe.wait_ge(s_zh, t + 1)
                    if after is not None:
                        pe.wait_ge(s_lt, after)
                for n in groups:
                    a, b = ZG[n]
                    if n == 2:
                        pe.wait_ge(s_zl, t + 1)
                    if n == 3:
                        pe.wait_ge(s_zt, t * 4 + 1)
                    for j in range(a, b):
                        c0 = CHUNKS[j % NCH]
                        src = zh if j < NCH else zl
                        last = pe.transpose(trp[n % 3][:, j - a, :], src[:, c0:c0 + P], ident[:, :])
                    last.then_inc(s_zp, 1)

            def tile(i, h, first, last):
                t = i * 2 + h
                new = first and h == 0
                pe.wait_ge(s_xt, t * 2 + 2)
                proj_in(t, h, "cq", 0, new)
                proj_in(t, h, "ckv", 1, new)
                proj_in(t, h, "aq", 2, new)
                if not new:
                    if not (first and h == 1):
                        pe.wait_ge(s_zt, t * 4 - 4)
                proj_in(t, h, "akv", 3, new)
                transpose_latents(t, new)
                proj_in(t, h, "ag", 4, new)
                pe.wait_ge(s_lt, t + 1)
                if new:
                    pe.wait_ge(s_whi, PIECE["ukv"])
                    pe.wait_ge(s_wlo, PIECE["ukv"])
                terms = []
                for k in range(3):
                    terms += [(latT[:, k, :], uq_hi[:, k, :]), (latT[:, k, :], uq_lo[:, k, :]), (latT[:, 3 + k, :], uq_hi[:, k, :])]
                project(t, 5, 384, terms, new)
                for n in range(2):
                    cols = slice(384 * n, 384 * n + 384)
                    terms = []
                    for k in range(2):
                        terms += [(latT[:, 6 + k, :], ukv_hi[:, k, cols]), (latT[:, 6 + k, :], ukv_lo[:, k, cols]),
                                  (latT[:, 8 + k, :], ukv_hi[:, k, cols])]
                    project(t, 6 + n, 384, terms, new)
                if not new:
                    transpose_z(t - 1, t + 1, (0, 1, 2))
                if not (last and h == 1):
                    transpose_x(t + 1, 1 - h)
                if not new:
                    transpose_z(t - 1, t + 1, (3,))
                proj_in(t, h, "bg", 8, new)

            pe.wait_ge(s_ident, 1)
            pe.wait_ge(s_ones, 4)
            transpose_x(0, 0)
            loop(pe, lambda i, first, last: [tile(i, h, first, last) for h in range(2)])
            transpose_z(TILES - 1, None, (0, 1, 2, 3))


def zero(t):
    return isinstance(t, int) and t == 0


def x_count(t, h):
    return (t - h) * 8 + 16


def phase2(nc, QA, KA, QBd, KBd, VA, VB, YA, YB, w_out, w_raw):
    STEPS = 8
    HALF = 3 * STEPS
    N = SEQ // QB * HB
    N32, NP = 4, 8
    PVLAG = 3
    PIECES = 4 * QT
    LEAD = 30
    PIECES_IN = [2, 2, 2, 0, 2, 2, 2, 0] + [2, 2, 0, 2, 2, 2, 0, 2] + [2, 3, 3, 3, 3, 2, 4, 4]
    ROUND = 3 * PIECES
    pieces_of = lambda s: list(range(LEAD + sum(PIECES_IN[:s]), LEAD + sum(PIECES_IN[:s + 1])))
    KW = 2 * QB
    ONE = 64.0
    with ExitStack() as ctx:
        sb = lambda n, s, d=F32: ctx.enter_context(nc.sbuf_tensor("p2_" + n, s, d))
        ps = lambda n, s, d=F32: ctx.enter_context(nc.psum_tensor("p2_" + n, s, d))
        sem = lambda n: ctx.enter_context(nc.semaphore("p2_" + n))

        ka_hl = [sb(f"ka_hl{g}", [P, SEQ], F16) for g in range(GA)]
        ka_h1 = [sb(f"ka_h1{g}", [66, SEQ], F16) for g in range(GA)]
        vas = sb("vas", [P, TILES, GA, 2 * DA + 1], F16)
        kb_h1 = sb("kb_h1", [DB + 2, SEQ], F16)
        kb_l = sb("kb_l", [DB, SEQ], F16)
        kb_m = sb("kb_m", [DB, SEQ], F16)
        qb_m = sb("qb_m", [DB, QB], F16)
        vbs = sb("vbs", [P, TILES, 2 * DVB + 1], F16)
        qa_hh = [sb(f"qa_hh{g}", [P, QB], F16) for g in range(GA)]
        qa_lm = [sb(f"qa_lm{g}", [66, QB], F16) for g in range(GA)]
        qb_h = sb("qb_h", [DB, QB], F16)
        qb_lm = sb("qb_lm", [DB + 2, QB], F16)
        p32 = sb("p32", [P, N32, KW])
        ph = sb("ph", [P, NP, 2, QB], F16)
        pl = sb("pl", [P, NP, 2, QB], F16)
        part = sb("part", [P, 2, PIECES])
        rowmax = sb("rowmax", [P, 2, QT])
        mpair = sb("mpair", [P, 2, QT, 2], F16)
        eye = sb("eye", [P, P], F16)
        acc_sb = sb("acc_sb", [P, QT, 2 * DA + 1])
        rden = sb("rden", [P, QT])
        ysum = sb("ysum", [P, QT, DVB])
        yout = sb("yout", [P, 2, QT, DVB])

        mx = ps("mx", [P, 2, QB])
        st = ps("st", [P, 2, 2, QB])
        acc = ps("acc", [P, 2, 512])
        accv = acc[:, :, 0:258].rearrange("p b (j c) -> p b j c", j=2)

        s_ka = [sem(f"ka_loaded{g}") for g in range(GA)]
        s_va = sem("va_loaded")
        s_q = [sem(f"q_loaded{p}") for p in range(3)]
        s_kb = sem("kb_loaded")
        s_bm = sem("b_max_loaded")
        s_vb = sem("vb_loaded")
        s_const = sem("constants")
        s_eye = sem("eye_ready")
        s_mx = sem("max_scores")
        s_red = sem("max_reduced")
        s_md = sem("max_chain")
        s_mt = sem("max_turned")
        s_mr = sem("max_rows")
        s_st = sem("scores")
        s_exp = sem("exp_done")
        s_hi = sem("p_hi")
        s_lo = sem("p_lo")
        s_pv = sem("pv_done")
        s_acc = sem("acc_copied")
        s_rden = sem("rden")
        s_y = sem("y_chain")
        s_yst = sem("y_stored")
        s_wout = sem("w_out_loaded")

        UNITS = [(0, "a"), (1, "a"), (0, "b")]

        def y_before(i, pos):
            return i * 5 + 2 * pos

        def turned(s, last):
            for e in pieces_of(s - 1) if s else ():
                if e % PIECES == 3 and not (last and e // PIECES > 3):
                    return e
            return None

        def before(i, s, act_on, first):
            pos = s // STEPS - 1
            act_on(i if pos >= 0 else i - 1, pos % 3, first and pos == 0)

        def loop(eng, body):
            body(0, True, False)
            with eng.Fori(1, N - 1) as i:
                body(i, False, False)
            body(N - 1, False, True)

        block = ctx.enter_context(nc.Block())

        @block.sync
        def _(sp):
            def load_q(i, pos):
                g, kind = UNITS[pos]
                if kind == "a":
                    for s, dsts in ((0, (qa_hh[g][0:64, :], qa_hh[g][64:128, :])), (1, (qa_lm[g][0:64, :],))):
                        src = QA[s].rearrange("(g h) (q two) r t -> g (h q) r two t", g=GA, two=2)[g, i]
                        for dst in dsts:
                            sp.dma_start(dst.rearrange("r (two t) -> r two t", two=2), src).then_inc(s_q[pos], 16)
                else:
                    for s, dst in enumerate((qb_h[:, :], qb_lm[0:DB, :])):
                        src = QBd[s].rearrange("h (q two) r t -> (h q) r two t", two=2)[i]
                        sp.dma_start(dst.rearrange("r (two t) -> r two t", two=2), src).then_inc(s_q[pos], 16)

            def load_kb(h):
                for s, dst in enumerate((kb_h1[0:DB, :], kb_l[:, :])):
                    sp.dma_start(dst.rearrange("r (pr t) -> r pr t", pr=PAIRS),
                                 KBd[s, h].rearrange("pr r t -> r pr t")).then_inc(s_kb, 16)

            def load_bm(i, h):
                sp.dma_start(kb_m[:, :].rearrange("r (pr t) -> r pr t", pr=PAIRS),
                             KBd[0, h].rearrange("pr r t -> r pr t")).then_inc(s_bm, 16)
                sp.dma_start(qb_m[:, :].rearrange("r (two t) -> r two t", two=2),
                             QBd[0].rearrange("h (q two) r t -> (h q) r two t", two=2)[i]).then_inc(s_bm, 16)

            def load_vb(h):
                sp.dma_start(vbs[:, :, :], VB.rearrange("t p h c -> h p t c")[h]).then_inc(s_vb, 16)

            def store_y(i, pos):
                sp.wait_ge(s_y, y_before(i, pos) + (2 if pos < 2 else 1))
                g, kind = UNITS[pos]
                if kind == "a":
                    sp.dma_start(YA[g].rearrange("h (q j) p d -> (h q) p j d", j=QT)[i], yout[:, pos % 2, :, 0:DA]).then_inc(s_yst, 16)
                else:
                    sp.dma_start(YB.rearrange("h (q j) p d -> (h q) p j d", j=QT)[i], yout[:, pos % 2, :, :]).then_inc(s_yst, 16)

            for g in range(GA):
                for s, dsts in ((0, (ka_hl[g][0:64, :], ka_h1[g][0:64, :])), (1, (ka_hl[g][64:128, :],))):
                    for dst in dsts:
                        sp.dma_start(dst.rearrange("r (pr t) -> r pr t", pr=PAIRS),
                                     KA[s, g].rearrange("pr r t -> r pr t")).then_inc(s_ka[g], 16)
                load_q(0, g)
            load_bm(0, 0)
            load_kb(0)
            load_q(0, 2)
            sp.dma_start(vas[:, :, :, :], VA.rearrange("t p g c -> p t g c")).then_inc(s_va, 16)
            load_vb(0)
            sp.dma_start(w_raw[:, :, :], w_out.rearrange("l (k p) n -> (l p) k n", p=P)).then_inc(s_wout, 16)

            def body(i, h):
                for pos in range(3):
                    sp.wait_ge(s_st, i * HALF + (pos + 1) * STEPS)
                    load_q(i + 1, pos)
                    if pos == 1:
                        sp.wait_ge(s_mx, (i + 1) * ROUND)
                        load_bm(i + 1, h)
                    if pos < 2:
                        store_y(i, pos)
                load_kb(h)
                sp.wait_ge(s_pv, i * HALF + HALF)
                load_vb(h)
                store_y(i, 2)

            for h in range(HB):
                with sp.Fori(max(h * NQ - 1, 0), h * NQ + NQ - 1) as i:
                    body(i, h)
            for pos in range(3):
                store_y(N - 1, pos)
            sp.wait_ge(s_yst, N * 48)
            sp.wait_ge(s_wout, 16)

        @block.gpsimd
        def _(pool):
            pool.memset(eye[:, :], 0.0).then_inc(s_eye, 1)
            pool.wait_ge(s_eye, 1)
            pool.affine_select(out=eye[:, :], in_=eye[:, :], compare_op=ALU.not_equal, fill=1.0,
                               base=0, pattern=[[-1, P]], channel_multiplier=1).then_inc(s_eye, 1)

            def unit(i, pos, first):
                u = i * 3 + pos
                kind = UNITS[pos][1]
                w = DA if kind == "a" else DVB
                if kind == "a":
                    pool.wait_ge(s_acc, u + 1)
                    pool.tensor_tensor(ysum[:, :, 0:w], acc_sb[:, :, 0:DA], acc_sb[:, :, DA:2 * DA], ALU.add).then_inc(s_y, 1)
                    src = ysum[:, :, 0:w]
                    pool.wait_ge(s_y, y_before(i, pos) + 1)
                else:
                    pool.wait_ge(s_acc, u + 1)
                    src = acc_sb[:, :, 0:w]
                pool.wait_ge(s_rden, u + 1)
                if not (first and pos == 0):
                    pool.wait_ge(s_yst, u * 16)
                pool.tensor_tensor(yout[:, pos % 2, :, 0:w], src, rden[:, :].unsqueeze(2).to_broadcast([P, QT, w]),
                                   ALU.mult).then_inc(s_y, 1)

            loop(pool, lambda i, first, last: [unit(i, pos, first) for pos in range(3)])

        @block.scalar
        def _(act):
            def copy_acc(i, pos, first):
                act.wait_ge(s_pv, i * HALF + pos * STEPS + STEPS)
                if not first:
                    act.wait_ge(s_y, y_before(i, pos))
                act.activation(acc_sb[:, :, :].rearrange("p (b j) c -> p b j c", b=2), accv, ACT.Copy).then_inc(s_acc, 1)

            def step(i, s, first):
                n = i * HALF + s
                scale = float(1.0 / np.sqrt(DA if UNITS[s // STEPS][1] == "a" else DB))
                act.wait_ge(s_st, n + 1)
                if not (first and s < N32):
                    act.wait_ge(s_lo, n + 1 - N32)
                act.activation(p32[:, s % N32, :], st[:, s % 2, :, :].rearrange("p a b -> p (a b)"), ACT.Exp,
                               scale=scale).then_inc(s_exp, 1)
                act.wait_ge(s_exp, n + 1)
                if not (first and s < NP):
                    act.wait_ge(s_pv, n + 1 - NP)
                act.activation(ph[:, s % NP, :, :].rearrange("p a b -> p (a b)"), p32[:, s % N32, :], ACT.Copy).then_inc(s_hi, 1)

            def body(i, first, last):
                for s in range(HALF):
                    step(i, s, first)
                    if s % STEPS == PVLAG - 1 and not (first and s < STEPS):
                        before(i, s, copy_acc, first)

            loop(act, body)
            copy_acc(N - 1, 2, False)

        @block.vector
        def _(dve):
            def reduce(e, c, upar, n):
                dve.wait_ge(s_mx, e + n)
                dve.tensor_reduce(part[:, upar, c:c + n], mx[:, c % 2:c % 2 + n, :], AX, ALU.max).then_inc(s_red, n)

            def max_done(u, upar):
                dve.wait_ge(s_red, (u + 1) * PIECES)
                dve.tensor_reduce(rowmax[:, upar, :], part[:, upar, :].rearrange("p (j k) -> p j k", k=4), AX, ALU.max).then_inc(s_md, 1)
                dve.wait_ge(s_md, u * 3 + 1)
                dve.tensor_scalar(mpair[:, upar, :, 0], rowmax[:, upar, :], -1.0 / ONE, None, ALU.mult).then_inc(s_md, 1)
                dve.wait_ge(s_md, u * 3 + 2)
                dve.scalar_tensor_tensor(out=mpair[:, upar, :, 1], in0=rowmax[:, upar, :], scalar=-1.0 / ONE,
                                         in1=mpair[:, upar, :, 0], op0=ALU.mult, op1=ALU.subtract).then_inc(s_md, 1)

            def rows(u, pos):
                g, kind = UNITS[pos]
                dve.wait_ge(s_mt, u + 1)
                if kind == "a":
                    dve.tensor_copy(qa_lm[g][64:66, :], mx[64:66, 0, :]).then_inc(s_mr, 1)
                else:
                    dve.tensor_copy(qb_lm[DB:DB + 2, :], mx[DB:DB + 2, 0, :]).then_inc(s_mr, 1)

            def lo(i, s, first):
                n = i * HALF + s
                dve.wait_ge(s_hi, n + 1)
                if not (first and s < NP):
                    dve.wait_ge(s_pv, n + 1 - NP)
                dve.tensor_tensor(pl[:, s % NP, :, :].rearrange("p a b -> p (a b)"), p32[:, s % N32, :],
                                  ph[:, s % NP, :, :].rearrange("p a b -> p (a b)"), ALU.subtract).then_inc(s_lo, 1)

            def ahead(i, e, last, n):
                pos, c = e // PIECES, e % PIECES
                if last and pos > 2:
                    return
                reduce(i * ROUND + e, c, pos % 3 % 2, n)
                if c + n == PIECES:
                    max_done(i * 3 + pos, pos % 3 % 2)

            def denominator(i, pos, first):
                dve.wait_ge(s_acc, i * 3 + pos + 1)
                if not first:
                    dve.wait_ge(s_y, y_before(i, pos))
                dve.reciprocal(rden[:, :], acc_sb[:, :, 2 * DA]).then_inc(s_rden, 1)

            def denominator_step(i, s, first):
                if s % STEPS == PVLAG + 1 and not (first and s < STEPS):
                    before(i, s, denominator, first)

            def body(i, first, last):
                for s in range(HALF):
                    es = pieces_of(s)
                    n = 2 if s < 2 * STEPS else 1
                    turn = turned(s, last)
                    if turn is not None:
                        u = turn // PIECES - 1
                        rows(i * 3 + u, u % 3)
                        early = 0
                    else:
                        early = max(len(es) // 2, n) if es else 0
                    for e in es[0:early:n]:
                        ahead(i, e, last, n)
                    if not (first and s == 0):
                        lo(i, s - 1, first)
                    for e in es[early::n]:
                        ahead(i, e, last, n)
                    denominator_step(i, s, first)

            for g in range(GA):
                dve.memset(ka_h1[g][64:66, :], ONE).then_inc(s_const, 1)
            dve.memset(kb_h1[DB:DB + 2, :], ONE).then_inc(s_const, 1)
            for e in range(0, LEAD, 2):
                u, c = e // PIECES, e % PIECES
                reduce(e, c, u % 2, 2)
                if c + 2 == PIECES:
                    max_done(u, u % 2)
                if c == 2 and u == 1:
                    rows(0, 0)
            loop(dve, body)
            lo(N - 1, HALF - 1, False)
            denominator(N - 1, 2, False)

        @block.tensor
        def _(pe):
            def max_scores(pos, c, e, start):
                g, kind = UNITS[pos]
                if not start:
                    pe.wait_ge(s_red, e - 1)
                queries = slice(c // 4 * P, (c // 4 + 1) * P)
                keys = slice(c % 4 * QB, (c % 4 + 1) * QB)
                if kind == "a":
                    pe.matmul(mx[:, c % 2, :], qa_hh[g][:, queries], ka_hl[g][:, keys], start=True, stop=True).then_inc(s_mx, 1)
                else:
                    pe.matmul(mx[:, c % 2, :], qb_m[:, queries], kb_m[:, keys], start=True, stop=True).then_inc(s_mx, 1)

            def loaded(i, pos):
                if UNITS[pos][1] == "a":
                    pe.wait_ge(s_q[pos], i * 48 + 48)
                else:
                    pe.wait_ge(s_bm, i * 32 + 32)

            def turn(u, pos):
                kind = UNITS[pos][1]
                p0 = 64 if kind == "a" else DB
                pe.wait_ge(s_md, u * 3 + 3)
                for j in range(QT):
                    last = pe.matmul(mx[p0:p0 + 2, 0, j * P:(j + 1) * P], mpair[:, pos % 2, j, :], eye[:, :],
                                     start=True, stop=True)
                last.then_inc(s_mt, 1)

            def ahead(i, e, last):
                posn, c = e // PIECES, e % PIECES
                if last and posn > 2:
                    return
                if c == 0:
                    loaded(i + posn // 3, posn % 3)
                if c == 4:
                    pe.wait_ge(s_mr, i * 3 + posn)
                max_scores(posn % 3, c, i * ROUND + e, False)

            def turn_step(i, s, last):
                e = turned(s, last)
                if e is not None:
                    pe.wait_ge(s_red, i * ROUND + (min(e, ROUND) if last else e))
                    u = e // PIECES - 1
                    turn(i * 3 + u, u % 3)

            def scores(i, s, first, last, between):
                pos = s // STEPS
                g, kind = UNITS[pos]
                n = i * HALF + s
                if s % STEPS == 0:
                    pe.wait_ge(s_mr, i * 3 + pos + 1)
                    if kind == "b":
                        pe.wait_ge(s_kb, i * 32 + 32)
                        pe.wait_ge(s_q[pos], i * 32 + 32)
                if not (first and s < 2):
                    pe.wait_ge(s_exp, n - 1)
                for b in range(2):
                    if b == 1 and between is not None:
                        ahead(i, between, last)
                    k0 = (s % STEPS * 2 + b) * P
                    keys = slice(k0, k0 + P)
                    out = st[:, s % 2, b, :]
                    if kind == "a":
                        pe.matmul(out, ka_hl[g][:, keys], qa_hh[g][:, :], start=True, stop=False)
                        end = pe.matmul(out, ka_h1[g][:, keys], qa_lm[g][:, :], start=False, stop=True)
                    else:
                        pe.matmul(out, kb_h1[0:DB, keys], qb_h[:, :], start=True, stop=False)
                        pe.matmul(out, kb_l[:, keys], qb_h[:, :], start=False, stop=False)
                        end = pe.matmul(out, kb_h1[:, keys], qb_lm[:, :], start=False, stop=True)
                end.then_inc(s_st, 1)

            def pv(i, s, first, b):
                pos = s // STEPS
                g, kind = UNITS[pos % 3]
                n = i * HALF + s
                slot = s % NP
                k = s % STEPS
                if b == 0 and k == 0 and not (first and s == 0):
                    pe.wait_ge(s_acc, i * 3 + pos)
                if b == 0 and k == 0 and pos == 2:
                    pe.wait_ge(s_vb, i * 16 + 16)
                if b == 0:
                    pe.wait_ge(s_hi, n + 1)
                    pe.wait_ge(s_lo, n + 1)
                t = 2 * k + b
                for j in range(QT):
                    hi, lo = ph[:, slot, b, j * P:(j + 1) * P], pl[:, slot, b, j * P:(j + 1) * P]
                    a = accv[:, j // 2, j % 2, :]
                    new, end = t == 0 and j % 2 == 0, t == TILES - 1
                    if kind == "a":
                        pe.matmul(a, hi, vas[:, t, g, :], start=new, stop=False, skip_group_check=True)
                        last = pe.matmul(a[:, DA:], lo, vas[:, t, g, DA:], start=False, stop=end, skip_group_check=True)
                    else:
                        pe.matmul(a, hi, vbs[:, t, DVB:], start=new, stop=False, skip_group_check=True)
                        pe.matmul(a[:, 0:DVB], hi, vbs[:, t, 0:DVB], start=False, stop=False, skip_group_check=True)
                        last = pe.matmul(a, lo, vbs[:, t, DVB:], start=False, stop=end, skip_group_check=True)
                if b == 1:
                    last.then_inc(s_pv, 1)

            def body(i, first, last):
                for s in range(HALF):
                    es = pieces_of(s)
                    if turned(s, last) is not None:
                        after = [3] * len(es)
                    elif s < 2 * STEPS:
                        after = [1] * len(es)
                    else:
                        after = {2: [1, 2], 3: [1, 2, 3], 4: [0, 1, 2, 3]}[len(es)]
                    at = lambda k: [e for e, a in zip(es, after) if a == k]
                    scores(i, s, first, last, at(0)[0] if at(0) else None)
                    turn_step(i, s, last)
                    for e in at(1):
                        ahead(i, e, last)
                    for b in range(2):
                        if not (first and s < PVLAG):
                            pv(i, s - PVLAG, first, b)
                        for e in at(2 + b):
                            ahead(i, e, last)

            pe.wait_ge(s_eye, 2)
            pe.wait_ge(s_const, 3)
            for e in range(LEAD):
                u, c = e // PIECES, e % PIECES
                if c == 0:
                    if UNITS[u][1] == "a":
                        pe.wait_ge(s_ka[u], 48)
                    loaded(0, u)
                if c == 4 and u == 1:
                    pe.wait_ge(s_mr, 1)
                max_scores(u, c, e, e < 2)
                if c == 3 and u == 1:
                    pe.wait_ge(s_red, e)
                    turn(0, 0)
            pe.wait_ge(s_va, 16)
            loop(pe, body)
            for s in range(HALF - PVLAG, HALF):
                for b in range(2):
                    pv(N - 1, s, False, b)


def phase3(nc, x, w_raw, YA, YB, G, out):
    WS = 64.0
    with ExitStack() as ctx:
        sb = lambda n, s, d=F32: ctx.enter_context(nc.sbuf_tensor("p3_" + n, s, d))
        ps = lambda n, s, d=F32: ctx.enter_context(nc.psum_tensor("p3_" + n, s, d))
        sem = lambda n: ctx.enter_context(nc.semaphore("p3_" + n))

        w_hi = sb("w_hi", [P, KT, D], F16)
        w_lo = sb("w_lo", [P, KT, D], F16)
        ya = sb("ya", [P, 2, HA, DA])
        yb = sb("yb", [P, 2, HB, DVB])
        gt = sb("gt", [P, 2, D])
        sg = sb("sg", [P, 2, D])
        xr = sb("xr", [P, 2, D])
        yg = sb("yg", [P, 2, D])
        yh = sb("yh", [P, D], F16)
        yl = sb("yl", [P, D], F16)
        yT = sb("yT", [P, 2, 2, KT, P], F16)
        res = sb("res", [P, 2, D])
        eye = sb("eye", [P, P], F16)
        tp = [ps(f"tp{s}", [P, KT, P], F16) for s in range(2)]
        po = [[ps(f"po{b}{c}", [P, 512]) for c in range(2)] for b in range(2)]

        s_whi = sem("w_hi")
        s_wlo = sem("w_lo")
        s_eye = sem("eye_ready")
        s_y = [sem("y_loaded0"), sem("y_loaded1")]
        s_g = [sem("g_loaded0"), sem("g_loaded1")]
        s_x = [sem("x_loaded0"), sem("x_loaded1")]
        s_sg = sem("silu_done")
        s_yg = sem("y_gated")
        s_yh = sem("y_hi")
        s_yl = sem("y_lo")
        s_tp = sem("yT_in_psum")
        s_yt = sem("yT_in_sbuf")
        s_po = sem("out_in_psum")
        s_res = sem("residual_added")
        s_out = [sem("out_stored0"), sem("out_stored1")]

        xt = x.rearrange("b (t p) d -> (b t) p d", p=P)
        ot = out.rearrange("b (t p) d -> (b t) p d", p=P)

        def loop(eng, body):
            for h in range(2):
                body(h, h, 0, True, False)
            with eng.Fori(1, PAIRS - 1) as i:
                for h in range(2):
                    body(i * 2 + h, h, i, False, False)
            for h in range(2):
                body(TILES - 2 + h, h, PAIRS - 1, False, True)

        block = ctx.enter_context(nc.Block())

        @block.sync
        def _(sp):
            def load_yg(t, h):
                for g in range(GA):
                    sp.dma_start(ya[:, h, g * 4:g * 4 + 4, :], YA[g].rearrange("h t p d -> t p h d")[t]).then_inc(s_y[h], 16)
                sp.dma_start(yb[:, h], YB.rearrange("h t p d -> t p h d")[t]).then_inc(s_y[h], 16)
                sp.dma_start(gt[:, h, :], G[t]).then_inc(s_g[h], 16)

            for t in range(2):
                load_yg(t, t)
            for t in range(2):
                sp.dma_start(xr[:, t, :], xt[t]).then_inc(s_x[t], 16)

            def tile(t, h, i, first, last):
                if not last:
                    sp.wait_ge(s_yg, t * 2 + 2)
                    load_yg(t + 2, h)
                sp.wait_ge(s_res, t * 2 + 2)
                sp.dma_start(ot[t], res[:, h, :]).then_inc(s_out[h], 16)
                if not last:
                    sp.dma_start(xr[:, h, :], xt[t + 2]).then_inc(s_x[h], 16)

            loop(sp, tile)
            for h in range(2):
                sp.wait_ge(s_out[h], PAIRS * 16)

        @block.gpsimd
        def _(pool):
            pool.memset(eye[:, :], 0.0).then_inc(s_eye, 1)
            pool.wait_ge(s_eye, 1)
            pool.affine_select(out=eye[:, :], in_=eye[:, :], compare_op=ALU.not_equal, fill=1.0,
                               base=0, pattern=[[-1, P]], channel_multiplier=1).then_inc(s_eye, 1)

        @block.scalar
        def _(act):
            def silu(t, h, i, early):
                act.wait_ge(s_g[h], i * 16 + 16)
                if not early:
                    act.wait_ge(s_yg, t * 2 - 2)
                act.activation(sg[:, h, :], gt[:, h, :], ACT.Silu).then_inc(s_sg, 1)

            def split_hi(c):
                for k in range(KT // 2):
                    ks, cols = slice(2 * k, 2 * k + 2), slice(c * 512, (c + 1) * 512)
                    act.activation(w_hi[:, ks, cols], w_raw[:, ks, cols], ACT.Copy, scale=WS).then_inc(s_whi, 1)

            split_hi(0)
            silu(0, 0, 0, True)

            def tile(t, h, i, first, last):
                act.wait_ge(s_yg, t * 2 + 2)
                if not (first and h == 0):
                    act.wait_ge(s_tp, t * 2)
                act.activation(yh[:, :], yg[:, h, :], ACT.Copy).then_inc(s_yh, 1)
                if first and h == 0:
                    split_hi(1)
                if not (last and h == 1):
                    silu(t + 1, 1 - h, i if h == 0 else i + 1, first and h == 0)
                for s in range(2):
                    act.wait_ge(s_tp, t * 2 + s + 1)
                    if not first:
                        act.wait_ge(s_po, t * 2 - 2)
                    act.activation(yT[:, h, s], tp[s][:, :, :], ACT.Copy).then_inc(s_yt, 1)

            loop(act, tile)

        @block.vector
        def _(dve):
            def gate(t, h, i, early):
                dve.wait_ge(s_y[h], i * 48 + 48)
                dve.wait_ge(s_sg, t + 1)
                if not early:
                    dve.wait_ge(s_yh, t - 1)
                    dve.wait_ge(s_yl, t - 1)
                dve.tensor_tensor(yg[:, h, 0:512], ya[:, h].rearrange("p h d -> p (h d)"), sg[:, h, 0:512], ALU.mult).then_inc(s_yg, 1)
                dve.tensor_tensor(yg[:, h, 512:], yb[:, h].rearrange("p h d -> p (h d)"), sg[:, h, 512:], ALU.mult).then_inc(s_yg, 1)

            def residual(t, h, i, early):
                for c in range(2):
                    cols = slice(c * 512, (c + 1) * 512)
                    dve.wait_ge(s_po, t * 2 + c + 1)
                    dve.wait_ge(s_x[h], i * 16 + 16)
                    if not early:
                        dve.wait_ge(s_out[h], i * 16)
                    dve.scalar_tensor_tensor(out=res[:, h, cols], in0=po[h][c][:, :], scalar=1.0 / WS, in1=xr[:, h, cols],
                                             op0=ALU.mult, op1=ALU.add).then_inc(s_res, 1)

            def split_lo(c):
                for k in range(KT // 2):
                    ks, cols = slice(2 * k, 2 * k + 2), slice(c * 512, (c + 1) * 512)
                    dve.wait_ge(s_whi, c * (KT // 2) + k + 1)
                    dve.scalar_tensor_tensor(out=w_lo[:, ks, cols], in0=w_raw[:, ks, cols], scalar=WS,
                                             in1=w_hi[:, ks, cols], op0=ALU.mult, op1=ALU.subtract).then_inc(s_wlo, 1)

            split_lo(0)
            gate(0, 0, 0, True)

            def tile(t, h, i, first, last):
                dve.wait_ge(s_yh, t + 1)
                if not (first and h == 0):
                    dve.wait_ge(s_tp, t * 2)
                dve.tensor_tensor(yl[:, :], yg[:, h, :], yh[:, :], ALU.subtract).then_inc(s_yl, 1)
                if first and h == 0:
                    split_lo(1)
                if not (last and h == 1):
                    gate(t + 1, 1 - h, i if h == 0 else i + 1, first and h == 0)
                if not (first and h == 0):
                    residual(t - 1, 1 - h, i - 1 if h == 0 else i, first or (isinstance(i, int) and i == 0))

            loop(dve, tile)
            residual(TILES - 1, 1, PAIRS - 1, False)

        @block.tensor
        def _(pe):
            def turn(t, first):
                for s, src in enumerate((yh, yl)):
                    pe.wait_ge(s_yh if s == 0 else s_yl, t + 1)
                    if not first:
                        pe.wait_ge(s_yt, t * 2 - 1 + s)
                    for k in range(KT):
                        last = pe.transpose(tp[s][:, k, :], src[:, k * P:(k + 1) * P], eye[:, :])
                    last.then_inc(s_tp, 1)

            def tile(t, h, i, first, last):
                pe.wait_ge(s_yt, t * 2 + 2)
                for c in range(2):
                    cols = slice(c * 512, (c + 1) * 512)
                    if not first:
                        pe.wait_ge(s_res, t * 2 - 3 + c)
                    for k in range(KT):
                        if first and h == 0 and k % 2 == 0:
                            pe.wait_ge(s_wlo, c * (KT // 2) + k // 2 + 1)
                        for m, (s, w) in enumerate(((0, w_hi), (0, w_lo), (1, w_hi))):
                            mm = pe.matmul(po[h][c][:, :], yT[:, h, s, k, :], w[:, k, cols],
                                           start=(k == 0 and m == 0), stop=(k == KT - 1 and m == 2))
                    mm.then_inc(s_po, 1)
                    if c == 0 and not (last and h == 1):
                        turn(t + 1, False)

            pe.wait_ge(s_eye, 2)
            turn(0, True)
            loop(pe, tile)


def layer(nc, x, w_in, w_uq, w_ukv, g_in, g_cq, g_ckv, g_heads, trig, eye, w_out, out):
    dram = lambda n, s, d=F16: nc.dram_tensor("scratch_" + n, s, d, kind="Internal").ap()
    QA = dram("qa", [2, HA, PAIRS, DA, 2 * P])
    KA = dram("ka", [2, GA, PAIRS, DA, 2 * P])
    QBd = dram("qb", [2, HB, PAIRS, DB, 2 * P])
    KBd = dram("kb", [2, HB, PAIRS, DB, 2 * P])
    VA = dram("va", [TILES, P, GA, 2 * DA + 1])
    VB = dram("vb", [TILES, P, HB, 2 * DVB + 1])
    G = dram("g", [TILES, P, D], F32)
    YA = dram("ya", [GA, HB, TILES, P, DA], F32)
    YB = dram("yb", [HB, TILES, P, DVB], F32)
    phase1(nc, x, w_in, w_uq, w_ukv, g_in, g_cq, g_ckv, g_heads, trig, eye, QA, KA, QBd, KBd, VA, VB, G)
    with nc.sbuf_tensor("w_out_raw", [P, KT, D], F32) as w_raw:
        phase2(nc, QA, KA, QBd, KBd, VA, VB, YA, YB, w_out, w_raw)
        phase3(nc, x, w_raw, YA, YB, G, out)


def kernel(**inputs):
    import concourse.bacc as _bacc
    from concourse.bass_utils import run_bass_kernel_spmd as _run

    a = {k: np.ascontiguousarray(v) for k, v in inputs.items()}
    heads = [a["a_q_norm"]] * HA + [a["a_k_norm"]] * GA + [a["b_q_norm"]] * HB + [a["b_k_norm"]] * HB
    named = {
        "x": a["x"], "w_in": a["w_in"], "w_uq": a["w_uq"], "w_ukv": a["w_ukv"], "g_in": a["norm_in"],
        "g_cq": a["b_cq_norm"], "g_ckv": a["b_ckv_norm"], "g_heads": np.concatenate(heads, axis=1).reshape(NZ),
        "trig": rope_tables(), "eye": np.eye(P, dtype=np.float32), "w_out": a["w_out"],
    }
    nc = _bacc.Bacc("TRN2", target_bir_lowering=False, num_devices=1)
    arrays, args = {}, []
    for name, v in named.items():
        arrays[f"in_{name}"] = v
        args.append(nc.dram_tensor(f"in_{name}", v.shape, mybir.dt.from_np(v.dtype), kind="ExternalInput").ap())
    args.append(nc.dram_tensor("out_0", (1, SEQ, D), F32, kind="ExternalOutput").ap())
    layer(nc, *args)
    r = _run(nc, [arrays], core_ids=[0])
    return r.results[0]["out_0"]
```
